# Optimizing a Trainium2 kernel written in Bass

```python
import jax
import jax.numpy as jnp
from jax import lax
import numpy as np

D_MODEL = 1024
BATCH = 1
SEQ = 256
DEPTH = 1

CHUNK = 64
Q_BLOCK = 128
HEAD_DIM = 64
N_HEADS_A = 8
N_HEADS_B = 8
N_IDX_HEADS = 8
IDX_DIM = 64
MAX_SELECTED_KEYS = 256
ROT_DIM = HEAD_DIM // 4
ROPE_THETA = 500000.0
N_EXPERTS = 32
TOP_K = 4
D_EXPERT = D_MODEL
SWIGLU_LIMIT = 7.0
SWIGLU_ALPHA = 1.702
EXPERT_BLOCK = 256
RMS_EPS = 1e-6
PROJ_WIDTHS = (N_HEADS_A * HEAD_DIM, HEAD_DIM, HEAD_DIM, N_IDX_HEADS * IDX_DIM, IDX_DIM, N_IDX_HEADS, N_HEADS_B * HEAD_DIM, N_HEADS_B * HEAD_DIM, N_HEADS_B * HEAD_DIM, D_MODEL, D_MODEL)
D_PROJ = sum(PROJ_WIDTHS)

kernel_name = 'hybrid_dsa_stickbreak_moe_block'

def split_points():
    pts, acc = [], 0
    for w in PROJ_WIDTHS[:-1]:
        acc += w
        pts.append(acc)
    return pts

def rms_norm(x, g):
    xf = x.astype(jnp.float32)
    y = xf * lax.rsqrt(jnp.mean(xf * xf, axis=-1, keepdims=True) + RMS_EPS)
    return (y * g.astype(jnp.float32)).astype(x.dtype)

def rope_tables(seq):
    pos = jnp.arange(seq, dtype=jnp.float32)
    inv_freq = ROPE_THETA ** (-jnp.arange(0, ROT_DIM, 2, dtype=jnp.float32) / ROT_DIM)
    ang = pos[:, None] * inv_freq[None, :]
    return jnp.cos(ang)[:, None, :], jnp.sin(ang)[:, None, :]

def partial_rope(x, cos, sin):
    half = ROT_DIM // 2
    x1 = x[..., :half].astype(jnp.float32)
    x2 = x[..., half:ROT_DIM].astype(jnp.float32)
    rot = jnp.concatenate([x1 * cos - x2 * sin, x2 * cos + x1 * sin], axis=-1).astype(x.dtype)
    return jnp.concatenate([rot, x[..., ROT_DIM:]], axis=-1)

def to_blocks(a):
    b, s = a.shape[:2]
    return jnp.moveaxis(a.reshape(b, s // Q_BLOCK, Q_BLOCK, *a.shape[2:]), 1, 0)

def from_blocks(a):
    nb, b, qb = a.shape[:3]
    return jnp.moveaxis(a, 0, 1).reshape(b, nb * qb, -1)

def dsa_attention(q, k, v, q_idx, k_idx, w_idx):
    s_len = q.shape[1]
    n_sel = min(MAX_SELECTED_KEYS, s_len // 4)
    key_pos = jnp.arange(s_len)

    def block(args):
        qb, qib, wb, bi = args
        t = bi * Q_BLOCK + jnp.arange(Q_BLOCK)
        limit = (t // CHUNK + 1) * CHUNK
        admissible = key_pos[None, :] < limit[:, None]
        rel = jax.nn.relu(jnp.einsum('bqhd,bsd->bqhs', qib, k_idx) * (IDX_DIM ** -0.5))
        score = jnp.einsum('bqhs,bqh->bqs', rel, wb).astype(jnp.float32)
        score = jnp.where(admissible[None], score, -jnp.inf)
        _, sel = lax.top_k(score, n_sel)
        valid = sel < limit[None, :, None]
        k_sel = jax.vmap(lambda kb, ib: kb[ib])(k, sel)
        v_sel = jax.vmap(lambda vb, ib: vb[ib])(v, sel)
        logits = jnp.einsum('bqhd,bqnd->bqhn', qb, k_sel).astype(jnp.float32) * (HEAD_DIM ** -0.5)
        logits = jnp.where(valid[:, :, None, :], logits, -jnp.inf)
        p = jax.nn.softmax(logits, axis=-1).astype(v.dtype)
        return jnp.einsum('bqhn,bqnd->bqhd', p, v_sel)

    nb = s_len // Q_BLOCK
    out = lax.map(block, (to_blocks(q), to_blocks(q_idx), to_blocks(w_idx), jnp.arange(nb)))
    return from_blocks(out)

def stick_breaking_attention(q, k, v):
    s_len = q.shape[1]
    key_pos = jnp.arange(s_len)

    def block(args):
        qb, bi = args
        t = bi * Q_BLOCK + jnp.arange(Q_BLOCK)
        causal = key_pos[None, :] < t[:, None]
        z = jnp.einsum('bqhd,bshd->bhqs', qb, k).astype(jnp.float32) * (HEAD_DIM ** -0.5)
        log_beta = jax.nn.log_sigmoid(z)
        log_keep = jnp.where(causal, jax.nn.log_sigmoid(-z), 0.0)
        later = lax.cumsum(log_keep, axis=3, reverse=True) - log_keep
        a = jnp.where(causal, jnp.exp(log_beta + later), 0.0).astype(v.dtype)
        return jnp.einsum('bhqs,bshd->bqhd', a, v)

    nb = s_len // Q_BLOCK
    out = lax.map(block, (to_blocks(q), jnp.arange(nb)))
    return from_blocks(out)

def hybrid_mixer(xn, w_in, q_norm_g, k_norm_g, w_proj_a, w_proj_b, w_out, cos, sin):
    b, s, _ = xn.shape
    proj = xn @ w_in
    qa, ka, va, qi, ki, wi, qb, kb, vb, ga, gb = jnp.split(proj, split_points(), axis=-1)
    qa = partial_rope(rms_norm(qa.reshape(b, s, N_HEADS_A, HEAD_DIM), q_norm_g), cos, sin)
    ka = partial_rope(rms_norm(ka.reshape(b, s, 1, HEAD_DIM), k_norm_g), cos, sin)[:, :, 0]
    qi = partial_rope(qi.reshape(b, s, N_IDX_HEADS, IDX_DIM), cos, sin)
    ki = partial_rope(ki.reshape(b, s, 1, IDX_DIM), cos, sin)[:, :, 0]
    wi = wi * (N_IDX_HEADS ** -0.5)
    oa = dsa_attention(qa, ka, va, qi, ki, wi)
    ob = stick_breaking_attention(qb.reshape(b, s, N_HEADS_B, HEAD_DIM), kb.reshape(b, s, N_HEADS_B, HEAD_DIM), vb.reshape(b, s, N_HEADS_B, HEAD_DIM))
    merged = jax.nn.sigmoid(ga) * (oa @ w_proj_a) + jax.nn.sigmoid(gb) * (ob @ w_proj_b)
    return merged @ w_out

def moe_ffn(xf, w_router, b_router, w_gu, b_gu, w_down, b_down):
    n, d = xf.shape
    logits = (xf @ w_router + b_router).astype(jnp.float32)
    top_vals, top_idx = lax.top_k(logits, TOP_K)
    gates = jax.nn.softmax(top_vals, axis=-1)
    m = n * TOP_K
    e_flat = top_idx.reshape(m)
    tok_flat = jnp.repeat(jnp.arange(n, dtype=jnp.int32), TOP_K)
    g_flat = gates.reshape(m)
    order = jnp.argsort(e_flat)
    e_sorted = e_flat[order]
    counts = jnp.bincount(e_flat, length=N_EXPERTS)
    padded = ((counts + EXPERT_BLOCK - 1) // EXPERT_BLOCK) * EXPERT_BLOCK
    start = jnp.cumsum(counts) - counts
    pend = jnp.cumsum(padded)
    pstart = pend - padded
    dest = pstart[e_sorted] + (jnp.arange(m) - start[e_sorted])
    n_blocks = (m + N_EXPERTS * (EXPERT_BLOCK - 1) + EXPERT_BLOCK - 1) // EXPERT_BLOCK
    rows = n_blocks * EXPERT_BLOCK
    tok_buf = jnp.zeros((rows,), jnp.int32).at[dest].set(tok_flat[order])
    gate_buf = jnp.zeros((rows,), xf.dtype).at[dest].set(g_flat[order].astype(xf.dtype))
    block_start = jnp.arange(n_blocks) * EXPERT_BLOCK
    block_expert = jnp.minimum(jnp.sum(pend[None, :] <= block_start[:, None], axis=1), N_EXPERTS - 1)
    x_blocks = xf[tok_buf].reshape(n_blocks, EXPERT_BLOCK, d)

    def expert_block(args):
        xb, e = args
        hgu = xb @ w_gu[e] + b_gu[e]
        gate = jnp.minimum(hgu[:, :D_EXPERT], SWIGLU_LIMIT)
        up = jnp.clip(hgu[:, D_EXPERT:], -SWIGLU_LIMIT, SWIGLU_LIMIT)
        act = (up + 1.0) * gate * jax.nn.sigmoid(SWIGLU_ALPHA * gate)
        return act @ w_down[e] + b_down[e]

    y_blocks = lax.map(expert_block, (x_blocks, block_expert)).reshape(rows, d)
    return jnp.zeros_like(xf).at[tok_buf].add(gate_buf[:, None] * y_blocks)

def setup_inputs(seed: int = 0) -> dict:
    key = jax.random.key(seed)
    ks = jax.random.split(key, 16)

    def normal(k, shape, scale):
        return jax.random.normal(k, shape, jnp.float32) * scale

    L = DEPTH
    wa = N_HEADS_A * HEAD_DIM
    wb = N_HEADS_B * HEAD_DIM
    return {
        'x': normal(ks[0], (BATCH, SEQ, D_MODEL), 1.0),
        'norm_mix_g': 1.0 + normal(ks[1], (L, D_MODEL), 0.02),
        'w_in': normal(ks[2], (L, D_MODEL, D_PROJ), D_MODEL ** -0.5),
        'q_norm_g': 1.0 + normal(ks[3], (L, HEAD_DIM), 0.02),
        'k_norm_g': 1.0 + normal(ks[4], (L, HEAD_DIM), 0.02),
        'w_proj_a': normal(ks[5], (L, wa, D_MODEL), wa ** -0.5),
        'w_proj_b': normal(ks[6], (L, wb, D_MODEL), wb ** -0.5),
        'w_out': normal(ks[7], (L, D_MODEL, D_MODEL), D_MODEL ** -0.5),
        'norm_ffn_g': 1.0 + normal(ks[8], (L, D_MODEL), 0.02),
        'w_router': normal(ks[9], (L, D_MODEL, N_EXPERTS), D_MODEL ** -0.5),
        'b_router': normal(ks[10], (L, N_EXPERTS), 0.01),
        'w_gate_up': normal(ks[11], (L, N_EXPERTS, D_MODEL, 2 * D_EXPERT), D_MODEL ** -0.5),
        'b_gate_up': normal(ks[12], (L, N_EXPERTS, 2 * D_EXPERT), 0.01),
        'w_down': normal(ks[13], (L, N_EXPERTS, D_EXPERT, D_MODEL), D_EXPERT ** -0.5),
        'b_down': normal(ks[14], (L, N_EXPERTS, D_MODEL), 0.01),
    }

def reference(x, norm_mix_g, w_in, q_norm_g, k_norm_g, w_proj_a, w_proj_b, w_out, norm_ffn_g, w_router, b_router, w_gate_up, b_gate_up, w_down, b_down):
    b, s, d = x.shape
    cos, sin = rope_tables(s)
    h = x
    for l in range(DEPTH):
        h = h + hybrid_mixer(rms_norm(h, norm_mix_g[l]), w_in[l], q_norm_g[l], k_norm_g[l], w_proj_a[l], w_proj_b[l], w_out[l], cos, sin)
        hn = rms_norm(h, norm_ffn_g[l]).reshape(b * s, d)
        h = h + moe_ffn(hn, w_router[l], b_router[l], w_gate_up[l], b_gate_up[l], w_down[l], b_down[l]).reshape(b, s, d)
    return h


_drawn_inputs = setup_inputs


def setup_inputs(seed=0):
    import zlib

    import numpy as np

    out = dict(_drawn_inputs(seed))
    spreads = {}
    factors = {'q_norm_g': 7.078, 'k_norm_g': 5.212, 'b_gate_up': 8.0, 'b_down': 8.0}
    for name, (base, spread) in spreads.items():
        noise = np.random.default_rng([zlib.crc32(name.encode()), seed]).standard_normal(out[name].shape)
        drawn = base * np.exp(spread * noise) if base else spread * noise
        out[name] = jnp.asarray(drawn.astype(out[name].dtype))
    for name, factor in factors.items():
        out[name] = (out[name] * factor).astype(out[name].dtype)
    return out
```

```python
from contextlib import ExitStack

import numpy as np

import concourse.bass as bass
from concourse import mybir

F32 = mybir.dt.float32
BF16 = mybir.dt.bfloat16
I32 = mybir.dt.int32
U32 = mybir.dt.uint32
ALU = mybir.AluOpType
ACT = mybir.ActivationFunctionType
AX_X = mybir.AxisListType.X

P = 128
D = 1024
KC = D // P
SEQ = 256
TB = SEQ // P
HD = 64
NH = 8
NP2 = NH // 2
SEL = 64
CHUNK = 64
ROT = 16
RH = ROT // 2
THETA = 500000.0
NE = 32
TOPK = 4
SLOTS = 64
FF = 1024
EPS = 1e-6
LIMIT = 7.0
ALPHA = 1.702
NEG = -1e30
TAKEN = -3e38
HSCALE = HD ** -0.5

QA, KA, VA, QI, KI, WI = 0, 512, 576, 640, 1152, 1216
QB, KB, VB, GA, GB = 1224, 1736, 2248, 2760, 3784
NTM = 1224

C_ID, C_LNEG, C_ONEG, C_STRICT, C_ONES = 0, 128, 256, 384, 512
C_SLOT, C_ADM, C_CAUSAL = 640, 768, 1280
C_COS, C_SINN, C_SIN, C_E32, C_OFF = 1664, 1696, 1712, 1728, 1760
C_EYE = 1764
C_W = 1796


def shape_constants():
    c = np.zeros((P, C_W), np.float32)
    p = np.arange(P)[:, None]
    q = np.arange(P)[None, :]
    c[:, C_ID:C_ID + P] = p == q
    c[:, C_LNEG:C_LNEG + P] = -1.0 * (p >= q)
    c[:, C_ONEG:C_ONEG + P] = -1.0
    c[:, C_STRICT:C_STRICT + P] = p < q
    c[:, C_ONES:C_ONES + P] = 1.0
    c[:, C_SLOT:C_SLOT + P] = np.arange(P)[None, :] % SLOTS
    for b in range(TB):
        t = b * P + p
        key = np.arange(SEQ)[None, :]
        c[:, C_ADM + b * SEQ:C_ADM + (b + 1) * SEQ] = np.where(key < (t // CHUNK + 1) * CHUNK, 0.0, NEG)
    diag = np.where(p < q, 0.0, NEG)
    c[:, C_CAUSAL:C_CAUSAL + P] = diag
    c[:, C_CAUSAL + 2 * P:C_CAUSAL + 3 * P] = diag
    freq = np.float32(THETA) ** (-np.arange(0, ROT, 2, dtype=np.float32) / np.float32(ROT))
    ang = np.arange(SEQ, dtype=np.float32)[:, None] * freq[None, :]
    cos, sin = np.cos(ang).astype(np.float32), np.sin(ang).astype(np.float32)
    for b in range(TB):
        rows = slice(b * P, (b + 1) * P)
        c[:, C_COS + b * ROT:C_COS + (b + 1) * ROT] = np.concatenate([cos[rows], cos[rows]], 1)
        c[:, C_SINN + b * RH:C_SINN + (b + 1) * RH] = -sin[rows]
        c[:, C_SIN + b * RH:C_SIN + (b + 1) * RH] = sin[rows]
    c[:, C_E32:C_E32 + NE] = np.arange(NE)[None, :]
    c[:, C_OFF:C_OFF + 4] = np.arange(4)[None, :] * SLOTS
    c[:, C_EYE:C_EYE + NE] = (p % NE == np.arange(NE)[None, :]) & (p < 3 * NE)
    return c


def hybrid_block(nc, x, norm_mix_g, w_in, q_norm_g, k_norm_g, w_proj_a, w_proj_b, w_out,
                 norm_ffn_g, w_router, b_router, w_gate_up, b_gate_up, w_down, b_down, consts, out):
    with ExitStack() as ctx:
        def sb(name, shape, dt=F32):
            return ctx.enter_context(nc.sbuf_tensor(name, shape, dt))

        def sem(name):
            return ctx.enter_context(nc.semaphore(name))

        ring = sb("ring", [P, 12 * 2048])
        unit = sb("unit", [P, 2, 4096])
        cst = sb("cst", [P, C_W])
        X = sb("X", [P, TB, D])
        XR = sb("XR", [P, TB, D])
        XT = sb("XT", [P, KC, SEQ])
        QAT = sb("QAT", [P, NP2, SEQ])
        KAT = sb("KAT", [P, SEQ])
        VBt = sb("VBt", [P, TB, 512])
        G = sb("G", [P, KC, 2, SEQ])
        SC = sb("SC", [P, TB, SEQ])
        MB = sb("MB", [P, TB, SEQ])
        OAT = sb("OAT", [P, NP2, SEQ])
        OBT = sb("OBT", [P, NP2, SEQ])
        bias3 = sb("bias3", [3 * NE, 2 * FF], BF16)
        BD = sb("BD", [NE, D])
        WR = sb("WR", [P, KC, NE])
        g_mix = sb("g_mix", [P, KC])
        g_ffn = sb("g_ffn", [P, KC])
        qg = sb("qg", [P, 2, HD])
        br = sb("br", [P, NE])
        sm = sb("sm", [P, 160])

        def slot(s, a=0, n=2048):
            return ring[:, 2048 * s + a:2048 * s + a + n]

        QBT = slot(6, 0, 1024).rearrange("p (j t) -> p j t", j=NP2)
        KBT = slot(6, 1024, 1024).rearrange("p (j t) -> p j t", j=NP2)
        QIT = slot(7, 0, 1024).rearrange("p (j t) -> p j t", j=NP2)
        KIT = slot(7, 1024, 256)
        SPt = slot(7, 1280, 768).rearrange("p (r c) -> p r c", r=2)
        W1 = slot(8)
        W2 = slot(9)
        TM = ring[:, 2048 * 10:2048 * 10 + TB * NTM].rearrange("p (b n) -> p b n", b=TB)
        NT = ring[:, 23040:23808].rearrange("p (r c) -> p r c", r=2)
        ET = ring[:, 23808:24576].rearrange("p (r c) -> p r c", r=2)
        TMP = unit[:, 1, :]
        KD = G[:, 0, :, :]
        RT = OAT[:, 0:3, :]

        gflat = G[:, :, :, :].rearrange("p c r t -> p (c r t)")
        xT = gflat[:, 0:512].rearrange("p (k s) -> p k s", k=KC)
        gm, sg, u1, tu, actb, hTf, ysb = (gflat[:, 512 * i:512 * (i + 1)] for i in range(1, 8))
        hT = hTf.rearrange("p (c r s) -> p c r s", c=4, r=2)
        ofl = OAT[:, :, :].rearrange("p j t -> p (j t)")
        GT = ofl[:, 0:256]
        OH = ofl[:, 256:384].rearrange("p (b s) -> p b s", b=TB)
        PG = ofl[:, 384:640].rearrange("p (b s) -> p b s", b=TB)
        RK = ofl[:, 640:704].rearrange("p (e b) -> p e b", b=TB)
        GE = ofl[:, 704:768].rearrange("p (e b) -> p e b", b=TB)
        rkc, gtc = ofl[:, 768:770], ofl[:, 770:772]
        obf = OBT[:, :, :].rearrange("p j t -> p (j t)")
        EQ = obf[:, 0:256].rearrange("p (b k e) -> p b k e", b=TB, k=TOPK)
        GQ = obf[:, 256:512].rearrange("p (b k e) -> p b k e", b=TB, k=TOPK)
        LGT = obf[:, 512:576].rearrange("p (b e) -> p b e", b=TB)
        M8 = obf[:, 576:592].rearrange("p (b k) -> p b k", b=TB)
        IXF = obf[:, 592:608].rearrange("p (b k) -> p b k", b=TB)
        G4 = obf[:, 608:616].rearrange("p (b k) -> p b k", b=TB)
        AS = obf[:, 616:680].rearrange("p (b e) -> p b e", b=TB)
        GPAD = obf[:, 680:936].rearrange("p (b e) -> p b e", b=TB)
        GTT = SC[0:NE, 0, :]
        I8 = sb("I8", [P, TB, 8], U32)
        CNT = sb("CNT", [P, NE], I32)
        SELE = sb("SELE", [3 * NE, SLOTS], BF16)
        ONEB = sb("ONEB", [3 * NE, SLOTS], BF16)

        ident = cst[:, C_ID:C_ID + P]
        lneg = cst[:, C_LNEG:C_LNEG + P]
        oneg = cst[:, C_ONEG:C_ONEG + P]
        strict = cst[:, C_STRICT:C_STRICT + P]
        ones = cst[:, C_ONES:C_ONES + P]
        slots = cst[:, C_SLOT:C_SLOT + P]
        adm = cst[:, C_ADM:C_ADM + TB * SEQ].rearrange("p (b s) -> p b s", b=TB)
        causal = cst[:, C_CAUSAL:C_CAUSAL + 384]
        cosd = cst[:, C_COS:C_COS + TB * ROT].rearrange("p (b r) -> p b r", b=TB)
        sinn = cst[:, C_SINN:C_SINN + TB * RH].rearrange("p (b r) -> p b r", b=TB)
        sinp = cst[:, C_SIN:C_SIN + TB * RH].rearrange("p (b r) -> p b r", b=TB)
        e32 = cst[:, C_E32:C_E32 + NE]
        off = cst[:, C_OFF:C_OFF + 4]
        eye3 = cst[0:3 * NE, C_EYE:C_EYE + NE]

        Pp = ctx.enter_context(nc.psum_tensor("Pp", [P, 2, 512], F32))
        Ap = ctx.enter_context(nc.psum_tensor("Ap", [P, 4, 512], F32))
        Bp = ctx.enter_context(nc.psum_tensor("Bp", [P, 2, 512], F32))
        Gps, Ups, Yps, Tps = Pp[:, 0, :], Pp[:, 1, :], Bp[:, 0, :], Bp[:, 1, :]

        in_c, in_x, in_v, in_b, in_r = (sem(n) for n in ("in_c", "in_x", "in_v", "in_b", "in_r"))
        unit_in = [sem(f"unit_in{u}") for u in range(14)]
        unit_used = sem("unit_used")
        w_full = [sem(f"w_full{s}") for s in range(12)]
        w_used = sem("w_used")
        v_chain = sem("v_chain")
        a_chain = sem("a_chain")
        g_chain = sem("g_chain")
        bias_ok = sem("bias_ok")
        a_sq, v_ms, a_rt, v_xr = sem("a_sq"), sem("v_ms"), sem("a_rt"), sem("v_xr")
        m_xt, a_xt = sem("m_xt"), sem("a_xt")
        m_half, a_half = sem("m_half"), sem("a_half")
        v_roti, v_rota, v_msa, a_rta = sem("v_roti"), sem("v_rota"), sem("v_msa"), sem("a_rta")
        m_ti, v_ti, m_ta, v_ta = sem("m_ti"), sem("v_ti"), sem("m_ta"), sem("v_ta")
        m_sc, a_relu, v_sum = sem("m_sc"), sem("a_relu"), sem("v_sum")
        m_lg, v_lg, a_ex, v_pr = sem("m_lg"), sem("v_lg"), sem("a_ex"), sem("v_pr")
        m_pt, v_pt, m_pv, v_pv = sem("m_pt"), sem("v_pt"), sem("m_pv"), sem("v_pv")
        m_bz, a_bl, v_bs = sem("m_bz"), sem("a_bl"), sem("v_bs")
        m_bc, v_ba, a_bp, m_bv, a_bo = sem("m_bc"), sem("v_ba"), sem("a_bp"), sem("m_bv"), sem("a_bo")
        a_sig, m_mg, v_mg, m_wo, v_h = sem("a_sig"), sem("m_mg"), sem("v_mg"), sem("m_wo"), sem("v_h")
        m_lr, v_tk, a_ge, v_as, m_rk, v_rk = (sem(n) for n in ("m_lr", "v_tk", "a_ge", "v_as", "m_rk", "v_rk"))
        m_g, v_g = sem("m_g"), sem("v_g")
        d_oh, m_ga, d_xt, m_gu = sem("d_oh"), sem("m_ga"), sem("d_xt"), sem("m_gu")
        d_gm, a_sg, d_act, m_ht, d_ht = sem("d_gm"), sem("a_sg"), sem("d_act"), sem("m_ht"), sem("d_ht")
        d_loc = sem("d_loc")
        m_gt, a_gt, m_y, a_y = sem("m_gt"), sem("a_gt"), sem("m_y"), sem("a_y")
        m_end, v_out, outs = sem("m_end"), sem("v_out"), sem("outs")

        def cols(a, n):
            return w_in[0].rearrange("(k p) n -> p k n", p=P)[:, :, a:a + n]

        def rows(w, k0):
            return w[0].rearrange("(k p) n -> p k n", p=P)[:, k0:k0 + 4, :]

        def uview(u, n=512):
            return unit[:, u % 2, 0:8 * n].rearrange("p (k n) -> p k n", k=8)

        def urows(u):
            return unit[:, u % 2, :].rearrange("p (k n) -> p k n", k=4)

        units = [[(uview(0), cols(QI, 512))],
                 [(uview(1, 200)[:, :, 0:72], cols(KI, 72)), (uview(1, 200)[:, :, 72:200], cols(KA, 128))],
                 [(uview(2), cols(QA, 512))], [(uview(3), cols(QB, 512))], [(uview(4), cols(KB, 512))],
                 [(uview(5), cols(VB, 512))], [(uview(6), cols(GA, 512))], [(uview(7), cols(GA + 512, 512))],
                 [(uview(8), cols(GB, 512))], [(uview(9), cols(GB + 512, 512))],
                 [(urows(10), rows(w_proj_a, 0))], [(urows(11), rows(w_proj_b, 0))],
                 [(urows(12), rows(w_out, 0))], [(urows(13), rows(w_out, 4))]]

        def piece_src(e, s):
            if s < 8:
                return w_gate_up[0, e, s * P:(s + 1) * P, :]
            r = (s - 8) * 2 * P
            return w_down[0, e, r:r + 2 * P, :].rearrange("(k p) n -> p k n", p=P)

        def piece_dst(s):
            return slot(s) if s < 8 else slot(s).rearrange("p (k n) -> p k n", k=2)

        block = ctx.enter_context(nc.Block())

        @block.sync
        def _(sp):
            sp.dma_start(cst[:, :], consts).then_inc(in_c, 16)
            for b in range(TB):
                sp.dma_start(X[:, b, :], x[0, b * P:(b + 1) * P, :]).then_inc(in_x, 16)
            for u, parts in enumerate(units):
                if u >= 2:
                    sp.wait_ge(unit_used, u - 1)
                if u == 1:
                    sp.wait_ge(a_xt, 8)
                for dst, src in parts:
                    sp.dma_start(dst, src).then_inc(unit_in[u], 16)
                if u == 3:
                    for s in range(3):
                        sp.dma_start(W2[32 * s:32 * s + 32, :], b_gate_up[0]).then_inc(in_b, 16)
                    sp.dma_start(BD[:, :], b_down[0]).then_inc(in_r, 16)
                    sp.dma_start(WR[:, :, :], w_router[0].rearrange("(k p) n -> p k n", p=P)).then_inc(in_r, 16)
                if u == 9:
                    for s in range(6):
                        sp.dma_start(piece_dst(s), piece_src(0, s)).then_inc(w_full[s], 16)
            sp.wait_ge(v_pv, 2)
            sp.wait_ge(a_bo, NP2)
            sp.wait_ge(m_bv, NP2)
            for s in range(6, 12):
                sp.dma_start(piece_dst(s), piece_src(0, s)).then_inc(w_full[s], 16)
            with sp.Fori(1, NE) as e:
                for s in range(12):
                    sp.wait_ge(w_used, (e - 1) * 12 + (s + 1))
                    sp.dma_start(piece_dst(s), piece_src(e, s)).then_inc(w_full[s], 16)
            for b in range(TB):
                sp.wait_ge(v_out, b + 1)
                sp.dma_start(out[0, b * P:(b + 1) * P, :], XR[:, b, :]).then_inc(outs, 16)
            sp.wait_ge(outs, 32)

        @block.gpsimd
        def _(pool):
            with nc.allow_non_contiguous_dma(reason="1024 gains, one per partition and chunk"):
                pool.dma_start(g_mix[:, :], norm_mix_g[0].rearrange("(k p) -> p k", p=P)).then_inc(in_v, 16)
                pool.dma_start(g_ffn[:, :], norm_ffn_g[0].rearrange("(k p) -> p k", p=P)).then_inc(in_v, 16)
            pool.dma_start(qg[:, 0, :], q_norm_g.partition_broadcast(P)[:, 0, :]).then_inc(in_v, 16)
            pool.dma_start(qg[:, 1, :], k_norm_g.partition_broadcast(P)[:, 0, :]).then_inc(in_v, 16)
            pool.dma_start(br[:, :], b_router.partition_broadcast(P)[:, 0, :]).then_inc(in_v, 16)
            nc.gpsimd.memset(ONEB[:, :], 1.0).then_inc(bias_ok, 1)
            pool.wait_ge(in_b, 48)
            n = 0
            for j in range(3):
                for q in range(j, 3):
                    r = slice(32 * q, 32 * q + 32)
                    if j:
                        nc.gpsimd.tensor_tensor(W2[r, :], W2[r, :], bias3[r, :], ALU.subtract).then_inc(g_chain, 1)
                        n += 1
                        pool.wait_ge(g_chain, n)
                    ins = nc.gpsimd.tensor_copy(bias3[r, :], W2[r, :])
                    if q == 2 and j == 2:
                        ins.then_inc(bias_ok, 1)
                    else:
                        ins.then_inc(g_chain, 1)
                        n += 1
                        pool.wait_ge(g_chain, n)

        @block.tensor
        def _(pe):
            mm, tr = nc.tensor.matmul, nc.tensor.transpose
            nhalf = [0]

            def half_bank():
                h = nhalf[0]
                if h >= 2:
                    pe.wait_ge(a_half, h - 1)
                return Pp[:, h % 2, :]

            def close_half(ins, last_of_unit):
                ins.then_inc(m_half, 1)
                nhalf[0] += 1
                if last_of_unit:
                    pe.wait_ge(m_half, nhalf[0])
                    pe.sem_inc(unit_used, 1)

            def token_half(u, b, n):
                if b == 0:
                    pe.wait_ge(unit_in[u], 16 * len(units[u]))
                bank = half_bank()
                for k in range(KC):
                    last = mm(bank[:, 0:n], XT[:, k, b * P:(b + 1) * P], uview(u, n)[:, k, :],
                              start=k == 0, stop=k == KC - 1)
                close_half(last, b == 1)

            def column_half(u, hf):
                if hf == 0:
                    pe.wait_ge(unit_in[u], 16)
                bank = half_bank()
                for t in range(2):
                    for k in range(KC):
                        c = (2 * hf + t) * P
                        last = mm(bank[:, t * SEQ:(t + 1) * SEQ], uview(u)[:, k, c:c + P], XT[:, k, :],
                                  start=k == 0, stop=k == KC - 1)
                close_half(last, hf == 1)

            pe.wait_ge(in_c, 16)
            pe.wait_ge(v_xr, 2)
            for b in range(TB):
                for k in range(KC):
                    last = tr(Ap[:, k // 2, (k % 2) * SEQ + b * P:(k % 2) * SEQ + (b + 1) * P],
                              XR[:, b, k * P:(k + 1) * P], ident)
            last.then_inc(m_xt, 1)
            pe.wait_ge(a_xt, 8)
            for u, n in ((0, 512), (1, 200), (2, 512)):
                for b in range(TB):
                    token_half(u, b, n)

            def query_key_transposes(q0, kbank):
                for b in range(TB):
                    for j in range(NP2):
                        tr(Ap[:, q0 + j // 2, (j % 2) * SEQ + b * P:(j % 2) * SEQ + (b + 1) * P],
                           TM[:, b, (QI if q0 == 0 else QA) + j * P:][:, 0:P], ident)
                    last = tr(kbank[:, b * P:(b + 1) * P], KD[:, b, 0:P] if q0 == 0 else KD[:, b, P:2 * P], ident)
                return last

            pe.wait_ge(v_roti, 1)
            query_key_transposes(0, Ap[:, 2, :]).then_inc(m_ti, 1)

            def head_products(qT, kT, b, base, nk):
                for j in range(NP2):
                    for r in range(2):
                        h = slice(64 * r, 64 * r + 64)
                        if nk == SEQ:
                            dst = Ap[:, 2 * r + j // 2, (j % 2) * SEQ:(j % 2 + 1) * SEQ]
                        else:
                            dst = Ap[:, base + r, j * P:(j + 1) * P]
                        last = mm(dst, qT[h, j, b * P:(b + 1) * P], kT[h, 0:nk], start=True, stop=True)
                return last

            def b_logits(p):
                if p >= 1:
                    pe.wait_ge(a_bo, p)
                for r in range(2):
                    h = slice(64 * r, 64 * r + 64)
                    mm(Bp[:, r, 0:SEQ], KBT[h, p, 0:P], QBT[h, p, :], start=True, stop=False, skip_group_check=True)
                for r in range(2):
                    h = slice(64 * r, 64 * r + 64)
                    last = mm(Bp[:, r, SEQ:384], KBT[h, p, P:SEQ], QBT[h, p, P:SEQ], start=False, stop=False,
                              skip_group_check=True)
                last.then_inc(m_bz, 1)

            def b_sums(p):
                pe.wait_ge(v_bs, p + 1)
                for r in range(2):
                    mm(Bp[:, r, 0:384], lneg, SPt[:, r, :], start=False, stop=False, skip_group_check=True)
                    last = mm(Bp[:, r, P:SEQ], oneg, SPt[:, r, SEQ:384], start=False, stop=True,
                              skip_group_check=True)
                last.then_inc(m_bc, 1)

            def b_values(p):
                pe.wait_ge(a_bp, p + 1)
                for r in range(2):
                    c = slice((2 * p + r) * HD, (2 * p + r + 1) * HD)
                    mm(Bp[64 * r:64 * r + 64, 0, 0:SEQ], VBt[:, 0, c], ET[:, r, 0:SEQ], start=True, stop=False,
                       skip_group_check=True)
                for r in range(2):
                    c = slice((2 * p + r) * HD, (2 * p + r + 1) * HD)
                    last = mm(Bp[64 * r:64 * r + 64, 0, P:SEQ], VBt[:, 1, c], ET[:, r, SEQ:384], start=False,
                              stop=True, skip_group_check=True)
                last.then_inc(m_bv, 1)

            column_half(3, 0)
            pe.wait_ge(v_ti, 1)
            head_products(QIT, KIT, 1, 0, SEQ).then_inc(m_sc, 1)
            column_half(3, 1)
            column_half(4, 0)
            pe.wait_ge(a_relu, 1)
            head_products(QIT, KIT, 0, 0, P).then_inc(m_sc, 1)
            pe.wait_ge(v_rota, 1)
            query_key_transposes(2, Bp[:, 0, :]).then_inc(m_ta, 1)
            column_half(4, 1)
            token_half(5, 0, 512)
            pe.wait_ge(a_relu, 2)
            pe.wait_ge(v_ta, 1)
            head_products(QAT, KAT, 1, 0, SEQ).then_inc(m_lg, 1)
            pe.wait_ge(a_half, 10)
            b_logits(0)
            token_half(5, 1, 512)
            b_sums(0)
            column_half(6, 0)
            pe.wait_ge(a_half, 12)
            b_values(0)
            b_logits(1)
            column_half(6, 1)
            b_sums(1)
            pe.wait_ge(v_pr, 1)
            for r in range(2):
                for kb in range(2):
                    for j in range(NP2):
                        last = tr(Ap[:, 2 * r + kb, j * P:(j + 1) * P],
                                  W1[:, (r * 4 + j) * SEQ + kb * P:(r * 4 + j) * SEQ + (kb + 1) * P], ident)
            last.then_inc(m_pt, 1)
            column_half(7, 0)
            b_values(1)
            b_logits(2)
            pe.wait_ge(v_pt, 1)
            for kb in range(2):
                for r in range(2):
                    last = mm(Ap[64 * r:64 * r + 64, 0, :], TM[:, kb, VA:VA + HD],
                              W2[:, (2 * r + kb) * 512:(2 * r + kb + 1) * 512], start=kb == 0, stop=kb == 1,
                              skip_group_check=True)
            last.then_inc(m_pv, 1)
            head_products(QAT, KAT, 0, 2, P).then_inc(m_lg, 1)
            column_half(7, 1)
            b_sums(2)
            column_half(8, 0)
            b_values(2)
            b_logits(3)
            pe.wait_ge(v_pr, 2)
            pe.wait_ge(v_pv, 1)
            for r in range(2):
                for j in range(NP2):
                    last = tr(Ap[:, r, j * P:(j + 1) * P], W1[:, (r * 4 + j) * P:(r * 4 + j + 1) * P], ident)
            last.then_inc(m_pt, 1)
            column_half(8, 1)
            b_sums(3)
            pe.wait_ge(v_pt, 2)
            for r in range(2):
                last = mm(Ap[64 * r:64 * r + 64, 2, :], TM[:, 0, VA:VA + HD], W2[:, r * 512:(r + 1) * 512],
                          start=True, stop=True, skip_group_check=True)
            last.then_inc(m_pv, 1)
            column_half(9, 0)
            b_values(3)
            column_half(9, 1)

            pe.wait_ge(v_pv, 2)
            pe.wait_ge(a_bo, NP2)
            pe.wait_ge(unit_in[10], 16)
            pe.wait_ge(unit_in[11], 16)
            for c in range(KC):
                if c >= 2:
                    pe.wait_ge(v_mg, c - 1)
                else:
                    pe.wait_ge(a_half, nhalf[0] - 1 + c)
                for ab, (u, o) in enumerate(((10, OAT), (11, OBT))):
                    for j in range(NP2):
                        last = mm(Pp[:, c % 2, ab * SEQ:(ab + 1) * SEQ], urows(u)[:, j, c * P:(c + 1) * P],
                                  o[:, j, :], start=j == 0, stop=j == NP2 - 1)
                last.then_inc(m_mg, 1)
            pe.wait_ge(m_mg, KC)
            pe.sem_inc(unit_used, 2)
            for c in range(KC):
                pe.wait_ge(v_mg, c + 1)
                if c % 4 == 0:
                    pe.wait_ge(unit_in[12 + c // 4], 16)
                for b in range(TB):
                    for hf in range(2):
                        last = mm(Ap[:, 2 * b + hf, :], XT[:, c, b * P:(b + 1) * P],
                                  urows(12 + c // 4)[:, c % 4, hf * 512:(hf + 1) * 512],
                                  start=c == 0, stop=c == KC - 1)
            last.then_inc(m_wo, 1)
            pe.wait_ge(v_xr, 4)
            for b in range(TB):
                for k in range(KC):
                    last = tr(Ap[:, k // 2, (k % 2) * SEQ + b * P:(k % 2) * SEQ + (b + 1) * P],
                              XR[:, b, k * P:(k + 1) * P], ident)
            last.then_inc(m_xt, 1)
            pe.wait_ge(a_xt, 16)
            pe.wait_ge(in_r, 32)
            for b in range(TB):
                for k in range(KC):
                    last = mm(Pp[:, 0, b * NE:(b + 1) * NE], XT[:, k, b * P:(b + 1) * P], WR[:, k, :],
                              start=k == 0, stop=k == KC - 1)
            last.then_inc(m_lr, 1)
            pe.wait_ge(v_as, 1)
            mm(Pp[:, 1, 0:NE], strict, AS[:, 0, :], start=True, stop=True)
            mm(Pp[:, 1, NE:2 * NE], ones, AS[:, 0, :], start=True, stop=False)
            mm(Pp[:, 1, NE:2 * NE], strict, AS[:, 1, :], start=False, stop=True)
            mm(Pp[:, 1, 2 * NE:3 * NE], ones, AS[:, 0, :], start=True, stop=False)
            mm(Pp[:, 1, 2 * NE:3 * NE], ones, AS[:, 1, :], start=False, stop=True).then_inc(m_rk, 1)
            for b in range(TB):
                last = tr(Bp[:, 0, b * P:(b + 1) * P], GPAD[:, b, :], ident)
            last.then_inc(m_g, 1)
            pe.wait_ge(v_g, 1)
            for b in range(TB):
                for hf in range(2):
                    mm(Ap[:, 2 * b + hf, :], GTT[:, b * P:(b + 1) * P], BD[:, hf * 512:(hf + 1) * 512],
                       start=True, stop=False, skip_group_check=True)

            def scatter():
                for b in range(TB):
                    for hf in range(2):
                        h = slice(64 * hf, 64 * hf + 64)
                        last = mm(Ap[:, 2 * b + hf, :], GT[h, b * P:(b + 1) * P], ysb[h, :],
                                  start=False, stop=False, skip_group_check=True)
                return last

            def expert_block(n, e, release):
                pe.wait_ge(d_oh, n)
                pe.wait_ge(a_gt, n)
                for k in range(KC):
                    for b in range(TB):
                        last = mm(Tps[:, k * SLOTS:(k + 1) * SLOTS], XR[:, b, k * P:(k + 1) * P], OH[:, b, :],
                                  start=b == 0, stop=b == 1)
                last.then_inc(m_ga, 1)
                pe.wait_ge(d_xt, n)
                for q in range(4):
                    mm((Gps, Ups)[q // 2][64 * (q % 2):64 * (q % 2) + 64, :], SELE[:, :],
                       bias3[:, q * 512:(q + 1) * 512], start=True, stop=False, skip_group_check=True)
                for k in range(KC):
                    pe.wait_ge(w_full[k], (e + 1) * 16)
                    for q in range(4):
                        last = mm((Gps, Ups)[q // 2][64 * (q % 2):64 * (q % 2) + 64, :], xT[:, k, :],
                                  slot(k, q * 512, 512), start=False, stop=k == KC - 1, skip_group_check=True)
                    if release and k < KC - 1:
                        last.then_inc(w_used, 1)
                last.then_inc(m_gu, 1)
                pe.wait_ge(a_y, n)
                last = scatter()
                if release:
                    last.then_inc(w_used, 1)
                for b in range(TB):
                    last = tr(Tps[:, b * P:(b + 1) * P], PG[:, b, :], ident)
                last.then_inc(m_gt, 1)
                pe.wait_ge(d_act, n)
                for c in range(4):
                    last = tr(Yps[:, c * P:(c + 1) * P], actb[:, c * P:(c + 1) * P], ident)
                last.then_inc(m_ht, 1)
                pe.wait_ge(d_ht, n)
                for s in range(4):
                    pe.wait_ge(w_full[8 + s], (e + 1) * 16)
                    for i in range(2):
                        k = 2 * s + i
                        for hf in range(2):
                            last = mm(Yps[64 * hf:64 * hf + 64, :], hT[:, k % 4, k // 4, :],
                                      slot(8 + s, i * 1024 + hf * 512, 512), start=k == 0, stop=k == KC - 1,
                                      skip_group_check=True)
                    if release and s < 3:
                        last.then_inc(w_used, 1)
                last.then_inc(m_y, 1)
                if release:
                    pe.wait_ge(m_y, n)
                    pe.sem_inc(w_used, 1)

            pe.wait_ge(bias_ok, 2)
            pe.wait_ge(v_rk, 1)
            extra = pe.alloc_register("pe_extra")
            pe.reg_mov(extra, 1)
            with pe.Fori(0, NE) as e:
                count = pe.value_load(CNT[0:1, bass.ds(e, 1)], min_val=0, max_val=SEQ)
                with pe.If(count > SLOTS):
                    with pe.Fori(1, SEQ // SLOTS) as j:
                        expert_block(pe.snap(extra) + e + (j - 1), e, False)
                    pe.reg_add(extra, extra, SEQ // SLOTS - 1)
                expert_block(pe.snap(extra) + e, e, True)
            pe.wait_ge(a_y, pe.snap(extra) + NE)
            pe.wait_ge(a_gt, pe.snap(extra) + NE)
            scatter().then_inc(m_end, 1)

        @block.vector
        def _(dve):
            V = nc.vector
            chain = [0]

            def link(ins):
                chain[0] += 1
                ins.then_inc(v_chain, 1)
                dve.wait_ge(v_chain, chain[0])

            def rsqrt(ss, n, width, ms_sem, rt_sem, count):
                v, s, y, t = (sm[:, i * 20:i * 20 + n] for i in range(1, 5))
                link(V.tensor_scalar(v, ss, 1.0 / width, EPS, ALU.mult, ALU.add))
                dve.sem_inc(ms_sem, 1)
                dve.wait_ge(rt_sem, count)
                link(V.reciprocal(y, s))
                link(V.tensor_tensor(t, y, y, ALU.mult))
                link(V.tensor_tensor(t, t, v, ALU.mult))
                link(V.tensor_scalar(t, t, -0.5, 1.5, ALU.mult, ALU.add))
                link(V.tensor_tensor(y, y, t, ALU.mult))
                return y

            def rotate(view, nheads):
                tmp = RT.rearrange("p a t -> p (a t)")[:, 0:2 * TB * nheads * ROT].rearrange(
                    "p (z b h r) -> p z b h r", z=2, b=TB, h=nheads)
                for b in range(TB):
                    cb = cosd[:, b:b + 1, :].to_broadcast([P, nheads, ROT])
                    nb = sinn[:, b:b + 1, :].to_broadcast([P, nheads, RH])
                    pb = sinp[:, b:b + 1, :].to_broadcast([P, nheads, RH])
                    V.tensor_tensor(tmp[:, 0, b], view[:, b, :, 0:ROT], cb, ALU.mult)
                    V.tensor_tensor(tmp[:, 1, b, :, 0:RH], view[:, b, :, RH:ROT], nb, ALU.mult)
                    link(V.tensor_tensor(tmp[:, 1, b, :, RH:ROT], view[:, b, :, 0:RH], pb, ALU.mult))
                for b in range(TB):
                    last = V.tensor_tensor(view[:, b, :, 0:ROT], tmp[:, 0, b], tmp[:, 1, b], ALU.add)
                return last

            dve.wait_ge(a_sq, 2)
            y = rsqrt(sm[:, 0:2], 2, D, v_ms, a_rt, 1)
            for b in range(TB):
                V.tensor_scalar(XR[:, b, :], X[:, b, :], y[:, b:b + 1], None, ALU.mult).then_inc(v_xr, 1)

            dve.wait_ge(a_half, 4)
            dve.wait_ge(in_c, 16)
            qi9 = TM[:, :, QI:QI + 9 * HD].rearrange("p b (h d) -> p b h d", h=9)
            link(rotate(qi9, 9))
            for b in range(TB):
                last = V.tensor_copy(KD[:, b, 0:P].rearrange("p (r d) -> p r d", r=2),
                                     TM[:, b:b + 1, KI:KI + HD].to_broadcast([P, 2, HD]))
            wis = sm[:, 100:116].rearrange("p (b h) -> p b h", b=TB)
            link(last)
            link(V.tensor_scalar(wis, TM[:, :, WI:WI + NH], NH ** -0.5, None, ALU.mult))
            dve.sem_inc(v_roti, 1)

            dve.wait_ge(a_half, 6)
            dve.wait_ge(in_v, 80)
            link(V.tensor_scalar(qg[:, 0, :], qg[:, 0, :], HSCALE, None, ALU.mult))
            for b in range(TB):
                qk = TM[:, b, 0:9 * HD]
                link(V.tensor_tensor(MB[:, :, :].rearrange("p b s -> p (b s)")[:, 0:512], qk[:, 0:512], qk[:, 0:512],
                                     ALU.mult))
                V.tensor_reduce(sm[:, 120 + 9 * b:128 + 9 * b],
                                MB[:, :, :].rearrange("p b s -> p (b s)").rearrange("p (h d) -> p h d", h=NH),
                                AX_X, ALU.add)
                link(V.tensor_tensor(SC[:, 0, 0:HD], qk[:, 512:576], qk[:, 512:576], ALU.mult))
                link(V.tensor_reduce(sm[:, 128 + 9 * b:129 + 9 * b], SC[:, 0, 0:HD], AX_X, ALU.add))
            y = rsqrt(sm[:, 120:138], 18, HD, v_msa, a_rta, 1)
            for b in range(TB):
                q9 = TM[:, b, 0:9 * HD].rearrange("p (h d) -> p h d", h=9)
                link(V.tensor_tensor(q9, q9, y[:, 9 * b:9 * b + 9].unsqueeze(2).to_broadcast([P, 9, HD]), ALU.mult))
                V.tensor_tensor(q9[:, 0:8, :], q9[:, 0:8, :], qg[:, 0:1, :].to_broadcast([P, 8, HD]), ALU.mult)
                link(V.tensor_tensor(q9[:, 8:9, :], q9[:, 8:9, :], qg[:, 1:2, :], ALU.mult))
            dve.wait_ge(m_ti, 1)
            V.tensor_copy(QIT, Ap[:, 0:2, :].rearrange("p a (j t) -> p (a j) t", j=2))
            V.tensor_copy(KIT, Ap[:, 2, 0:SEQ]).then_inc(v_ti, 1)
            link(rotate(TM[:, :, 0:9 * HD].rearrange("p b (h d) -> p b h d", h=9), 9))
            for b in range(TB):
                last = V.tensor_copy(KD[:, b, P:2 * P].rearrange("p (r d) -> p r d", r=2),
                                     TM[:, b:b + 1, KA:KA + HD].to_broadcast([P, 2, HD]))
            last.then_inc(v_rota, 1)

            def index_scores(b, nk, count):
                dve.wait_ge(a_relu, count)
                prev = adm[:, b, 0:nk]
                for j in range(NP2):
                    for r in range(2):
                        hh = r * 4 + j
                        link(V.scalar_tensor_tensor(out=SC[:, b, 0:nk], in0=W1[:, hh * nk:(hh + 1) * nk],
                                                    scalar=wis[:, b, 2 * j + r:2 * j + r + 1], in1=prev,
                                                    op0=ALU.mult, op1=ALU.add))
                        prev = SC[:, b, 0:nk]
                dve.sem_inc(v_sum, 1)

            def select_keys(b, nk):
                top = sm[:, 140:148]
                for _ in range(SEL // 8):
                    link(V.max(top, SC[:, b, 0:nk]))
                    link(V.match_replace(SC[:, b, 0:nk], top, SC[:, b, 0:nk], TAKEN))
                link(V.tensor_scalar(MB[:, b, 0:nk], SC[:, b, 0:nk], -2e38, NEG, ALU.is_gt, ALU.mult))

            def mask_logits(b, nk, src, count):
                dve.wait_ge(m_lg, count)
                L = W1[:, 0:NH * nk].rearrange("p (h s) -> p h s", h=NH)
                link(V.tensor_tensor(L, src, MB[:, b:b + 1, 0:nk].to_broadcast([P, NH, nk]), ALU.add))
                link(V.tensor_reduce(sm[:, 0:8], L, AX_X, ALU.max))
                V.tensor_scalar(sm[:, 8:16], sm[:, 0:8], -1.0, None, ALU.mult).then_inc(v_lg, 1)

            def normalise(nk, count):
                dve.wait_ge(a_ex, NH * count)
                link(V.reciprocal(sm[:, 148:156], sm[:, 80:88]))
                L = W1[:, 0:NH * nk].rearrange("p (h s) -> p h s", h=NH)
                V.tensor_tensor(L, L, sm[:, 148:156].unsqueeze(2).to_broadcast([P, NH, nk]), ALU.mult)\
                    .then_inc(v_pr, 1)

            def b_softplus(p):
                dve.wait_ge(a_bl, p + 1)
                link(V.scalar_tensor_tensor(out=SPt, in0=Bp[:, :, 0:384], scalar=0.0, in1=ET, op0=ALU.max, op1=ALU.add))
                for r in range(2):
                    d = SPt[:, r, :].rearrange("p (g q) -> p g q", g=3)[:, 0:3:2, :]
                    last = V.tensor_tensor(d, d, cst[:, C_STRICT:C_STRICT + P].unsqueeze(1).to_broadcast([P, 2, P]),
                                           ALU.mult)
                last.then_inc(v_bs, 1)

            def b_argument(p):
                dve.wait_ge(m_bc, p + 1)
                V.scalar_tensor_tensor(out=NT, in0=Bp[:, :, 0:384], scalar=0.0,
                                       in1=causal.unsqueeze(1).to_broadcast([P, 2, 384]),
                                       op0=ALU.min, op1=ALU.add).then_inc(v_ba, 1)

            index_scores(1, SEQ, 1)
            dve.wait_ge(m_ta, 1)
            V.tensor_copy(QAT[:, :, :], Ap[:, 2:4, :].rearrange("p a (j t) -> p (a j) t", j=2))
            V.tensor_copy(KAT[:, :], Bp[:, 0, 0:SEQ]).then_inc(v_ta, 1)
            select_keys(1, SEQ)
            index_scores(0, P, 2)
            dve.wait_ge(bias_ok, 2)
            mask_logits(1, SEQ, Ap[:, :, :].rearrange("p a (j s) -> p (a j) s", j=2), 1)
            b_softplus(0)
            normalise(SEQ, 1)
            b_argument(0)
            select_keys(0, P)
            b_softplus(1)
            dve.wait_ge(m_pt, 1)
            V.tensor_copy(W2, Ap[:, :, :].rearrange("p a n -> p (a n)")).then_inc(v_pt, 1)
            b_argument(1)
            dve.wait_ge(m_pv, 1)
            V.tensor_copy(OAT[:, :, P:SEQ], Ap[:, 0, :].rearrange("p (j q) -> p j q", j=NP2)).then_inc(v_pv, 1)
            mask_logits(0, P, Ap[:, 2:4, :].rearrange("p a (j s) -> p (a j) s", j=NP2), 2)
            b_softplus(2)
            normalise(P, 2)
            b_argument(2)
            dve.wait_ge(m_pt, 2)
            V.tensor_copy(W2[:, 0:1024], Ap[:, 0:2, :].rearrange("p a n -> p (a n)")).then_inc(v_pt, 1)
            b_softplus(3)
            dve.wait_ge(m_pv, 2)
            V.tensor_copy(OAT[:, :, 0:P], Ap[:, 2, :].rearrange("p (j q) -> p j q", j=NP2)).then_inc(v_pv, 1)
            b_argument(3)

            for c in range(KC):
                dve.wait_ge(m_mg, c + 1)
                dve.wait_ge(a_sig, c // 2 + 1)
                gc = G[:, c, :, :].rearrange("p r t -> p (r t)")
                link(V.tensor_tensor(gc, gc, Pp[:, c % 2, :], ALU.mult))
                V.tensor_tensor(XT[:, c, :], G[:, c, 0, :], G[:, c, 1, :], ALU.add).then_inc(v_mg, 1)
            dve.wait_ge(m_wo, 1)
            for b in range(TB):
                V.tensor_tensor(X[:, b, :], X[:, b, :], Ap[:, 2 * b:2 * b + 2, :].rearrange("p a n -> p (a n)"),
                                ALU.add).then_inc(v_h, 1)
            V.memset(GPAD, 0.0)
            V.memset(GT, 0.0)
            V.memset(ysb, 0.0)
            dve.wait_ge(a_sq, 4)
            y = rsqrt(sm[:, 0:2], 2, D, v_ms, a_rt, 2)
            for b in range(TB):
                V.tensor_scalar(XR[:, b, :], X[:, b, :], y[:, b:b + 1], None, ALU.mult).then_inc(v_xr, 1)
            dve.wait_ge(m_lr, 1)
            link(V.tensor_tensor(LGT, Pp[:, 0, 0:TB * NE].rearrange("p (b e) -> p b e", b=TB),
                                 br[:, :].unsqueeze(1).to_broadcast([P, TB, NE]), ALU.add))
            V.max(M8[:, 0, :], LGT[:, 0, :])
            link(V.max(M8[:, 1, :], LGT[:, 1, :]))
            V.max_index(I8[:, 0, :], M8[:, 0, :], LGT[:, 0, :])
            link(V.max_index(I8[:, 1, :], M8[:, 1, :], LGT[:, 1, :]))
            V.tensor_copy(IXF, I8[:, :, :])
            V.tensor_tensor(G4, M8[:, :, 0:TOPK], M8[:, :, 0:1].to_broadcast([P, TB, TOPK]),
                            ALU.subtract).then_inc(v_tk, 1)
            dve.wait_ge(a_ge, 1)
            link(V.tensor_reduce(sm[:, 0:2], G4, AX_X, ALU.add))
            link(V.reciprocal(sm[:, 2:4], sm[:, 0:2]))
            link(V.tensor_tensor(G4, G4, sm[:, 2:4].unsqueeze(2).to_broadcast([P, TB, TOPK]), ALU.mult))
            for b in range(TB):
                last = V.tensor_tensor(EQ[:, b], e32.unsqueeze(1).to_broadcast([P, TOPK, NE]),
                                       IXF[:, b, 0:TOPK].unsqueeze(2).to_broadcast([P, TOPK, NE]), ALU.is_equal)
            link(last)
            for b in range(TB):
                last = V.tensor_tensor(GQ[:, b], EQ[:, b], G4[:, b, :].unsqueeze(2).to_broadcast([P, TOPK, NE]),
                                       ALU.mult)
            link(last)
            for b in range(TB):
                V.tensor_reduce(AS[:, b, :], EQ[:, b].rearrange("p k e -> p e k"), AX_X, ALU.add)
                last = V.tensor_reduce(GPAD[:, b, 0:NE], GQ[:, b].rearrange("p k e -> p e k"), AX_X, ALU.add)
            link(last)
            dve.sem_inc(v_as, 1)
            V.tensor_copy(GE.rearrange("p e b -> p b e"), GPAD[:, :, 0:NE])
            dve.wait_ge(m_rk, 1)
            link(V.scalar_tensor_tensor(out=LGT, in0=Pp[:, 1, 0:TB * NE].rearrange("p (b e) -> p b e", b=TB),
                                        scalar=1.0, in1=AS, op0=ALU.add, op1=ALU.mult))
            link(V.tensor_scalar(RK.rearrange("p e b -> p b e"), LGT, -1.0, None, ALU.add))
            V.tensor_copy(CNT[:, :], Pp[:, 1, 2 * NE:3 * NE]).then_inc(v_rk, 1)
            dve.wait_ge(m_g, 1)
            V.tensor_copy(GTT, Bp[0:NE, 0, 0:SEQ]).then_inc(v_g, 1)

            def expert_block(n, e, offset):
                if offset is None:
                    V.tensor_copy(rkc, RK[:, bass.ds(e, 1), :].rearrange("p e b -> p (e b)"))
                else:
                    V.tensor_scalar(rkc, RK[:, bass.ds(e, 1), :].rearrange("p e b -> p (e b)"),
                                    off[:, bass.ds(offset, 1)], None, ALU.subtract)
                V.tensor_scalar(SELE[:, :], ONEB[:, :], eye3[:, bass.ds(e, 1)], None, ALU.mult)
                V.tensor_copy(gtc, GE[:, bass.ds(e, 1), :].rearrange("p e b -> p (e b)")).then_inc(d_loc, 1)
                dve.wait_ge(d_loc, n * 4 - 3)
                for b in range(TB):
                    V.tensor_scalar(OH[:, b, :], slots[:, 0:SLOTS], rkc[:, b:b + 1], None, ALU.is_equal)
                for b in range(TB):
                    last = V.tensor_scalar(PG[:, b, :], slots, rkc[:, b:b + 1], gtc[:, b:b + 1],
                                           ALU.is_equal, ALU.mult)
                last.then_inc(d_oh, 1)
                dve.wait_ge(m_ga, n)
                V.tensor_tensor(xT, Tps.rearrange("p (k s) -> p k s", k=KC),
                                g_ffn[:, :].unsqueeze(2).to_broadcast([P, KC, SLOTS]), ALU.mult).then_inc(d_xt, 1)
                dve.wait_ge(m_gu, n)
                V.tensor_scalar(gm, Gps, LIMIT, None, ALU.min).then_inc(d_gm, 1)
                V.tensor_scalar(u1, Ups, LIMIT, -LIMIT, ALU.min, ALU.max).then_inc(d_loc, 1)
                dve.wait_ge(d_loc, n * 4 - 2)
                V.scalar_tensor_tensor(out=tu, in0=u1, scalar=1.0, in1=gm, op0=ALU.add, op1=ALU.mult)\
                    .then_inc(d_loc, 1)
                dve.wait_ge(d_loc, n * 4 - 1)
                dve.wait_ge(a_sg, n)
                V.tensor_tensor(actb, tu, sg, ALU.mult).then_inc(d_act, 1)
                dve.wait_ge(m_ht, n)
                V.tensor_copy(hTf, Yps).then_inc(d_ht, 1)
                dve.sem_inc(d_loc, 1)

            dve.wait_ge(v_rk, 1)
            extra = dve.alloc_register("dve_extra")
            dve.reg_mov(extra, 1)
            with dve.Fori(0, NE) as e:
                count = dve.value_load(CNT[0:1, bass.ds(e, 1)], min_val=0, max_val=SEQ)
                with dve.If(count > SLOTS):
                    with dve.Fori(1, SEQ // SLOTS) as j:
                        expert_block(dve.snap(extra) + e + (j - 1), e, j)
                    dve.reg_add(extra, extra, SEQ // SLOTS - 1)
                expert_block(dve.snap(extra) + e, e, None)
            dve.wait_ge(m_end, 1)
            for b in range(TB):
                V.tensor_tensor(XR[:, b, :], X[:, b, :], Ap[:, 2 * b:2 * b + 2, :].rearrange("p a n -> p (a n)"),
                                ALU.add).then_inc(v_out, 1)

        @block.scalar
        def _(act):
            A = nc.scalar.activation

            def squares(count):
                for b in range(TB):
                    if count:
                        act.wait_ge(v_h, b + 1)
                    else:
                        act.wait_ge(in_x, 32)
                    A(XR[:, b, :], X[:, b, :], ACT.Square, accum_out=sm[:, b:b + 1]).then_inc(a_sq, 1)

            def root(n, ms_sem, rt_sem, count):
                act.wait_ge(ms_sem, count)
                A(sm[:, 40:40 + n], sm[:, 20:20 + n], ACT.Sqrt).then_inc(rt_sem, 1)

            def gained_transpose(gain, count):
                act.wait_ge(m_xt, count)
                for k in range(KC):
                    A(XT[:, k, :], Ap[:, k // 2, (k % 2) * SEQ:(k % 2 + 1) * SEQ], ACT.Copy,
                      scale=gain[:, k:k + 1]).then_inc(a_xt, 1)

            nh = [0]

            def evacuate(*parts):
                act.wait_ge(m_half, nh[0] + 1)
                bank = Pp[:, nh[0] % 2, :]
                for i, (dst, a, n, scale) in enumerate(parts):
                    src = bank[:, a:a + n]
                    if len(dst.shape) == 3:
                        src = src.rearrange("p (j t) -> p j t", t=dst.shape[2])
                    ins = A(dst, src, ACT.Copy, scale=scale)
                ins.then_inc(a_half, 1)
                nh[0] += 1

            squares(0)
            root(2, v_ms, a_rt, 1)
            act.wait_ge(in_v, 80)
            gained_transpose(g_mix, 1)
            for b in range(TB):
                evacuate((TM[:, b, QI:QI + 512], 0, 512, HSCALE))
            for b in range(TB):
                evacuate((TM[:, b, KI:KI + 72], 0, 72, 1.0), (TM[:, b, KA:KA + 128], 72, 128, 1.0))
            for b in range(TB):
                evacuate((TM[:, b, QA:QA + 512], 0, 512, 1.0))
            root(18, v_msa, a_rta, 1)

            def relu(b, n, count):
                act.wait_ge(m_sc, count)
                A(W1[:, 0:n], Ap[:, 0:n // 512, :].rearrange("p a n -> p (a n)"), ACT.Relu).then_inc(a_relu, 1)

            def b_log(p):
                act.wait_ge(m_bz, p + 1)
                A(ET, Bp[:, :, 0:384], ACT.Abs).then_inc(a_chain, 1)
                act.wait_ge(a_chain, 2 * p + 1)
                A(ET, ET, ACT.Exp, scale=-1.0).then_inc(a_chain, 1)
                act.wait_ge(a_chain, 2 * p + 2)
                A(ET, ET, ACT.Ln, bias=1.0).then_inc(a_bl, 1)

            def b_exp(p):
                act.wait_ge(v_ba, p + 1)
                A(ET, NT, ACT.Exp).then_inc(a_bp, 1)

            def b_out(p):
                act.wait_ge(m_bv, p + 1)
                A(OBT[:, p, :], Bp[:, 0, 0:SEQ], ACT.Copy).then_inc(a_bo, 1)

            def a_exp(nk, count):
                act.wait_ge(v_lg, count)
                for h in range(NH):
                    A(W1[:, h * nk:(h + 1) * nk], W1[:, h * nk:(h + 1) * nk], ACT.Exp, bias=sm[:, 8 + h:9 + h],
                      accum_out=sm[:, 80 + h:81 + h]).then_inc(a_ex, 1)

            def gate_half(u, hf):
                ab, c = (u - 6) // 2, 4 * ((u - 6) % 2) + 2 * hf
                evacuate((G[:, c:c + 2, ab, :], 0, 512, 1.0))

            evacuate((QBT[:, 0:2, :], 0, 512, HSCALE))
            relu(1, 2048, 1)
            evacuate((QBT[:, 2:4, :], 0, 512, HSCALE))
            evacuate((KBT[:, 0:2, :], 0, 512, 1.0))
            act.wait_ge(v_sum, 1)
            relu(0, 1024, 2)
            evacuate((KBT[:, 2:4, :], 0, 512, 1.0))
            evacuate((VBt[:, 0, :], 0, 512, 1.0))
            evacuate((VBt[:, 1, :], 0, 512, 1.0))
            b_log(0)
            a_exp(SEQ, 1)
            gate_half(6, 0)
            b_exp(0)
            b_out(0)
            gate_half(6, 1)
            b_log(1)
            gate_half(7, 0)
            b_exp(1)
            b_out(1)
            b_log(2)
            a_exp(P, 2)
            gate_half(7, 1)
            gate_half(8, 0)
            b_exp(2)
            b_out(2)
            b_log(3)
            gate_half(8, 1)
            gate_half(9, 0)
            b_exp(3)
            b_out(3)
            gate_half(9, 1)
            act.wait_ge(a_half, nh[0])
            for i in range(4):
                gi = G[:, 2 * i:2 * i + 2, :, :].rearrange("p c r t -> p (c r t)")
                A(gi, gi, ACT.Sigmoid).then_inc(a_sig, 1)
            squares(1)
            root(2, v_ms, a_rt, 2)
            gained_transpose(g_ffn, 2)
            act.wait_ge(v_tk, 1)
            A(G4, G4, ACT.Exp).then_inc(a_ge, 1)

            def expert_block(n):
                act.wait_ge(d_gm, n)
                A(sg, gm, ACT.Sigmoid, scale=ALPHA).then_inc(a_sg, 1)
                act.wait_ge(m_gt, n)
                A(GT, Tps[:, 0:SEQ], ACT.Copy).then_inc(a_gt, 1)
                act.wait_ge(m_y, n)
                A(ysb, Yps, ACT.Copy).then_inc(a_y, 1)

            act.wait_ge(v_rk, 1)
            act.sem_inc(a_gt, 1)
            act.sem_inc(a_y, 1)
            extra = act.alloc_register("act_extra")
            act.reg_mov(extra, 1)
            with act.Fori(0, NE) as e:
                count = act.value_load(CNT[0:1, bass.ds(e, 1)], min_val=0, max_val=SEQ)
                with act.If(count > SLOTS):
                    with act.Fori(1, SEQ // SLOTS) as j:
                        expert_block(act.snap(extra) + e + (j - 1))
                    act.reg_add(extra, extra, SEQ // SLOTS - 1)
                expert_block(act.snap(extra) + e)


_INS = ["x", "norm_mix_g", "w_in", "q_norm_g", "k_norm_g", "w_proj_a", "w_proj_b", "w_out", "norm_ffn_g",
        "w_router", "b_router", "w_gate_up", "b_gate_up", "w_down", "b_down"]


def kernel(**inputs):
    import concourse.bacc as bacc
    from concourse.bass_utils import run_bass_kernel_spmd

    nc = bacc.Bacc("TRN2", target_bir_lowering=False, num_devices=1)
    arrays, args = {}, []
    for name in _INS + ["consts"]:
        a = np.ascontiguousarray(inputs[name]) if name in inputs else shape_constants()
        arrays[f"in_{name}"] = a
        args.append(nc.dram_tensor(f"in_{name}", a.shape, mybir.dt.from_np(a.dtype), kind="ExternalInput").ap())
    args.append(nc.dram_tensor("out_h", (1, SEQ, D), F32, kind="ExternalOutput").ap())
    hybrid_block(nc, *args)
    r = run_bass_kernel_spmd(nc, [arrays], core_ids=[0])
    return r.results[0]["out_h"]
```

```python
from contextlib import ExitStack

import numpy as np

import concourse.bass as bass
from concourse import mybir

F32 = mybir.dt.float32
BF16 = mybir.dt.bfloat16
I32 = mybir.dt.int32
U32 = mybir.dt.uint32
ALU = mybir.AluOpType
ACT = mybir.ActivationFunctionType
AX_X = mybir.AxisListType.X

P = 128
D = 1024
KC = D // P
SEQ = 256
TB = SEQ // P
HD = 64
NH = 8
NP2 = NH // 2
SEL = 64
CHUNK = 64
ROT = 16
RH = ROT // 2
THETA = 500000.0
NE = 32
TOPK = 4
SLOTS = 64
PIECES = 12
PLACES = 18
OWN = 2
FF = 1024
EPS = 1e-6
LIMIT = 7.0
ALPHA = 1.702
NEG = -1e30
TAKEN = -3e38
HSCALE = HD ** -0.5

QA, KA, VA, QI, KI, WI = 0, 512, 576, 640, 1152, 1216
QB, KB, VB, GA, GB = 1224, 1736, 2248, 2760, 3784
NTM = 1224

C_ID, C_LNEG, C_ONEG, C_STRICT, C_ONES = 0, 128, 256, 384, 512
C_SLOT, C_ADM, C_CAUSAL = 640, 768, 1280
C_COS, C_SINN, C_SIN, C_E32, C_OFF = 1664, 1696, 1712, 1728, 1760
C_EYE = 1764
C_W = 1796


def shape_constants():
    c = np.zeros((P, C_W), np.float32)
    p = np.arange(P)[:, None]
    q = np.arange(P)[None, :]
    c[:, C_ID:C_ID + P] = p == q
    c[:, C_LNEG:C_LNEG + P] = -1.0 * (p >= q)
    c[:, C_ONEG:C_ONEG + P] = -1.0
    c[:, C_STRICT:C_STRICT + P] = p < q
    c[:, C_ONES:C_ONES + P] = 1.0
    c[:, C_SLOT:C_SLOT + P] = np.arange(P)[None, :] % SLOTS
    for b in range(TB):
        t = b * P + p
        key = np.arange(SEQ)[None, :]
        c[:, C_ADM + b * SEQ:C_ADM + (b + 1) * SEQ] = np.where(key < (t // CHUNK + 1) * CHUNK, 0.0, NEG)
    diag = np.where(p < q, 0.0, NEG)
    c[:, C_CAUSAL:C_CAUSAL + P] = diag
    c[:, C_CAUSAL + 2 * P:C_CAUSAL + 3 * P] = diag
    freq = np.float32(THETA) ** (-np.arange(0, ROT, 2, dtype=np.float32) / np.float32(ROT))
    ang = np.arange(SEQ, dtype=np.float32)[:, None] * freq[None, :]
    cos, sin = np.cos(ang).astype(np.float32), np.sin(ang).astype(np.float32)
    for b in range(TB):
        rows = slice(b * P, (b + 1) * P)
        c[:, C_COS + b * ROT:C_COS + (b + 1) * ROT] = np.concatenate([cos[rows], cos[rows]], 1)
        c[:, C_SINN + b * RH:C_SINN + (b + 1) * RH] = -sin[rows]
        c[:, C_SIN + b * RH:C_SIN + (b + 1) * RH] = sin[rows]
    c[:, C_E32:C_E32 + NE] = np.arange(NE)[None, :]
    c[:, C_OFF:C_OFF + 4] = np.arange(4)[None, :] * SLOTS
    c[:, C_EYE:C_EYE + NE] = (p % NE == np.arange(NE)[None, :]) & (p < 3 * NE)
    return c


def hybrid_block(nc, x, norm_mix_g, w_in, q_norm_g, k_norm_g, w_proj_a, w_proj_b, w_out,
                 norm_ffn_g, w_router, b_router, w_gate_up, b_gate_up, w_down, b_down, consts, out):
    with ExitStack() as ctx:
        def sb(name, shape, dt=F32):
            return ctx.enter_context(nc.sbuf_tensor(name, shape, dt))

        def sem(name):
            return ctx.enter_context(nc.semaphore(name))

        ring = sb("ring", [P, 12 * 2048])
        unit = sb("unit", [P, 2, 4096])
        cst = sb("cst", [P, C_W])
        X = sb("X", [P, TB, D])
        XR = sb("XR", [P, TB, D])
        XT = sb("XT", [P, KC, SEQ])
        qkv = sb("qkv", [P, 2304])
        QAT = qkv[:, 0:1024].rearrange("p (j t) -> p j t", j=NP2)
        VBt = qkv[:, 1024:2048].rearrange("p (b n) -> p b n", b=TB)
        KAT = qkv[:, 2048:2304]
        G = sb("G", [P, KC, 2, SEQ])
        att = sb("att", [P, 2048])
        SC = att[:, 0:512].rearrange("p (b t) -> p b t", b=TB)
        MB = att[:, 512:1024].rearrange("p (b t) -> p b t", b=TB)
        OAT = att[:, 1024:2048].rearrange("p (j t) -> p j t", j=NP2)
        OBT = sb("OBT", [P, NP2, SEQ])
        bias3 = sb("bias3", [3 * NE, 2 * FF], BF16)
        zero = sb("zero", [1, P + 512], BF16)
        WR = sb("WR", [P, KC, NE])
        gst = sb("gst", [2 * KC, P])
        gains = sb("gains", [P, 2 * KC])
        g_mix, g_ffn = gains[:, 0:KC], gains[:, KC:2 * KC]
        mhalf = sb("mhalf", [P, 18])
        qg = sb("qg", [P, 2, HD])
        br = sb("br", [P, NE])
        sm = sb("sm", [P, 160])

        def slot(s, a=0, n=2048):
            return ring[:, 2048 * s + a:2048 * s + a + n]

        QBT = slot(6, 0, 1024).rearrange("p (j t) -> p j t", j=NP2)
        KBT = slot(6, 1024, 1024).rearrange("p (j t) -> p j t", j=NP2)
        QIT = slot(7, 0, 1024).rearrange("p (j t) -> p j t", j=NP2)
        KIT = slot(7, 1024, 256)
        SPt = slot(7, 1280, 768).rearrange("p (r c) -> p r c", r=2)
        W1 = slot(8)
        W2 = slot(9)
        TM = ring[:, 2048 * 10:2048 * 10 + TB * NTM].rearrange("p (b n) -> p b n", b=TB)
        NT = ring[:, 23040:23808].rearrange("p (r c) -> p r c", r=2)
        ET = ring[:, 23808:24576].rearrange("p (r c) -> p r c", r=2)
        KD = G[:, 0, :, :]
        RT = OAT[:, 0:3, :]

        gflat = G[:, :, :, :].rearrange("p c r t -> p (c r t)")
        xTf = gm = hTf = gflat[:, 0:512]
        u1 = tu = actb = gflat[:, 512:1024]
        sg, ysb = gflat[:, 1024:1536], gflat[:, 1536:2048]
        xT = xTf.rearrange("p (k s) -> p k s", k=KC)
        hT = hTf.rearrange("p (c r s) -> p c r s", c=4, r=2)
        ofl = cst[:, C_ADM:C_COS]
        GT = ofl[:, 0:256]
        OH = ofl[:, 256:384].rearrange("p (b s) -> p b s", b=TB)
        PG = ofl[:, 384:640].rearrange("p (b s) -> p b s", b=TB)
        RK = ofl[:, 640:704].rearrange("p (e b) -> p e b", b=TB)
        GE = ofl[:, 704:768].rearrange("p (e b) -> p e b", b=TB)
        rkc, gtc = ofl[:, 768:770], ofl[:, 770:772]
        obf = OBT[:, :, :].rearrange("p j t -> p (j t)")
        EQ = obf[:, 0:256].rearrange("p (b k e) -> p b k e", b=TB, k=TOPK)
        GQ = obf[:, 256:512].rearrange("p (b k e) -> p b k e", b=TB, k=TOPK)
        LGT = obf[:, 512:576].rearrange("p (b e) -> p b e", b=TB)
        M8 = obf[:, 576:592].rearrange("p (b k) -> p b k", b=TB)
        IXF = obf[:, 592:608].rearrange("p (b k) -> p b k", b=TB)
        G4 = obf[:, 608:616].rearrange("p (b k) -> p b k", b=TB)
        AS = obf[:, 616:680].rearrange("p (b e) -> p b e", b=TB)
        GPAD = obf[:, 680:936].rearrange("p (b e) -> p b e", b=TB)
        I8 = sb("I8", [P, TB, 8], U32)
        CNT = sb("CNT", [P, NE + 1], I32)
        SELE = sb("SELE", [3 * NE, SLOTS], BF16)
        ONEB = sb("ONEB", [3 * NE, SLOTS], BF16)

        ident = cst[:, C_ID:C_ID + P]
        lneg = cst[:, C_LNEG:C_LNEG + P]
        oneg = cst[:, C_ONEG:C_ONEG + P]
        strict = cst[:, C_STRICT:C_STRICT + P]
        ones = cst[:, C_ONES:C_ONES + P]
        slots = cst[:, C_SLOT:C_SLOT + P]
        adm = cst[:, C_ADM:C_ADM + TB * SEQ].rearrange("p (b s) -> p b s", b=TB)
        causal = cst[:, C_CAUSAL:C_CAUSAL + 384]
        cosd = cst[:, C_COS:C_COS + TB * ROT].rearrange("p (b r) -> p b r", b=TB)
        sinn = cst[:, C_SINN:C_SINN + TB * RH].rearrange("p (b r) -> p b r", b=TB)
        sinp = cst[:, C_SIN:C_SIN + TB * RH].rearrange("p (b r) -> p b r", b=TB)
        e32 = cst[:, C_E32:C_E32 + NE]
        off = cst[:, C_OFF:C_OFF + 4]
        eye3 = cst[0:3 * NE, C_EYE:C_EYE + NE]

        Pp = ctx.enter_context(nc.psum_tensor("Pp", [P, 2, 512], F32))
        Ap = ctx.enter_context(nc.psum_tensor("Ap", [P, 4, 512], F32))
        Bp = ctx.enter_context(nc.psum_tensor("Bp", [P, 2, 512], F32))
        Gps, Ups, Yps, Tps = Pp[:, 0, :], Pp[:, 1, :], Bp[:, 0, :], Bp[:, 1, :]

        in_c, in_id, in_v, in_b, in_r = (sem(n) for n in ("in_c", "in_id", "in_v", "in_b", "in_r"))
        z_ok, y_zero, in_bd = sem("z_ok"), sem("y_zero"), sem("in_bd")
        in_x = [sem(f"in_x{b}") for b in range(TB)]
        unit_in = [sem(f"unit_in{u}") for u in range(14)]
        w_full = [sem(f"w_full{s}") for s in range(PLACES)]
        own_full = [sem(f"own_full{s}") for s in range(OWN)]
        w_used = sem("w_used")
        v_chain = sem("v_chain")
        a_chain = sem("a_chain")
        g_chain = sem("g_chain")
        bias_ok = sem("bias_ok")
        in_g, p_half, m_gn, a_gn = sem("in_g"), sem("p_half"), sem("m_gn"), sem("a_gn")
        a_sq, v_ms, p_rt, v_xr = sem("a_sq"), sem("v_ms"), sem("p_rt"), sem("v_xr")
        m_xt, a_xt, v_xt = sem("m_xt"), sem("a_xt"), sem("v_xt")
        m_half, a_half = sem("m_half"), sem("a_half")
        v_roti, v_rota = sem("v_roti"), sem("v_rota")
        m_ti, v_ti, m_ta, v_ta = sem("m_ti"), sem("v_ti"), sem("m_ta"), sem("v_ta")
        m_sc, a_relu, v_sum = sem("m_sc"), sem("a_relu"), sem("v_sum")
        m_lg, v_lg, a_ex, v_pr = sem("m_lg"), sem("v_lg"), sem("a_ex"), sem("v_pr")
        m_pt, v_pt, m_pv, v_pv = sem("m_pt"), sem("v_pt"), sem("m_pv"), sem("v_pv")
        m_bz, a_bl, v_bs = sem("m_bz"), sem("a_bl"), sem("v_bs")
        m_bc, v_ba, a_bp, m_bv, a_bo = sem("m_bc"), sem("v_ba"), sem("a_bp"), sem("m_bv"), sem("a_bo")
        a_sig, m_mg, v_mg, m_wo = sem("a_sig"), sem("m_mg"), sem("v_mg"), sem("m_wo")
        m_lr, v_tk, a_ge, v_as, m_rk, v_rk = (sem(n) for n in ("m_lr", "v_tk", "a_ge", "v_as", "m_rk", "v_rk"))
        m_g, a_g, v_gp = sem("m_g"), sem("a_g"), sem("v_gp")
        d_oh, m_ga, d_xt, m_gu = sem("d_oh"), sem("m_ga"), sem("d_xt"), sem("m_gu")
        d_gm, a_sg, d_act, m_ht, d_ht = sem("d_gm"), sem("a_sg"), sem("d_act"), sem("m_ht"), sem("d_ht")
        d_loc = sem("d_loc")
        m_gt, a_gt, m_y, a_y = sem("m_gt"), sem("a_gt"), sem("m_y"), sem("a_y")
        m_end, v_out, outs = sem("m_end"), sem("v_out"), sem("outs")

        def cols(a, n):
            return w_in[0].rearrange("(k p) n -> p k n", p=P)[:, :, a:a + n]

        def rows(w, k0):
            return w[0].rearrange("(k p) n -> p k n", p=P)[:, k0:k0 + 4, :]

        def uview(u, n=512):
            flat = slot(2, 0, 4096) if u == 2 else unit[:, u % 2, :]
            return flat[:, 0:8 * n].rearrange("p (k n) -> p k n", k=8)

        def urows(u):
            flat = unit[:, 0, :] if u == 10 else slot(2 * (u - 11), 0, 4096)
            return flat.rearrange("p (k n) -> p k n", k=4)

        units = [[(uview(0), cols(QI, 512))],
                 [(uview(1, 200)[:, :, 0:72], cols(KI, 72)), (uview(1, 200)[:, :, 72:200], cols(KA, 128))],
                 [(uview(2), cols(QA, 512))], [(uview(3), cols(QB, 512))], [(uview(4), cols(KB, 512))],
                 [(uview(5), cols(VB, 512))], [(uview(6), cols(GA, 512))], [(uview(7), cols(GA + 512, 512))],
                 [(uview(8), cols(GB, 512))], [(uview(9), cols(GB + 512, 512))],
                 [(urows(10), rows(w_proj_a, 0))], [(urows(11), rows(w_proj_b, 0))],
                 [(urows(12), rows(w_out, 0))], [(urows(13), rows(w_out, 4))]]

        def piece_src(e, s):
            if s < 8:
                return w_gate_up[0, e, s * P:(s + 1) * P, :]
            r = (s - 8) * 2 * P
            return w_down[0, e, r:r + 2 * P, :].rearrange("(k p) n -> p k n", p=P)

        place = [slot(s) for s in range(12)] + [
            unit[:, 1, 0:2048], unit[:, 1, 2048:4096], unit[:, 0, 0:2048], unit[:, 0, 2048:4096],
            qkv[:, 0:2048], XT[:, :, :].rearrange("p k t -> p (k t)")]
        own_place = [att[:, :], gflat[:, 2048:4096]]

        def place_of(i, s):
            if i < 0:
                if s >= PIECES - OWN:
                    return own_place[s - (PIECES - OWN)], own_full[s - (PIECES - OWN)], 1
                return place[s], w_full[s], 1
            r = PIECES * (i + 1) + s - OWN
            return place[r % PLACES], w_full[r % PLACES], r // PLACES + 1

        block = ctx.enter_context(nc.Block())

        @block.sync
        def _(sp):
            for b in range(TB):
                sp.dma_start(X[:, b, :], x[0, b * P:(b + 1) * P, :]).then_inc(in_x[b], 16)
            sp.dma_start(ident, consts[:, C_ID:C_ID + P]).then_inc(in_id, 16)

            def load_unit(u):
                for dst, src in units[u]:
                    sp.dma_start(dst, src).then_inc(unit_in[u], 16)

            for u in range(11):
                if u >= 3:
                    sp.wait_ge(m_half, 4 if u == 3 else 2 if u == 4 else 2 * (u - 1))
                load_unit(u)
                if u == 0:
                    sp.dma_start(cst[:, P:], consts[:, P:]).then_inc(in_c, 16)
                if u == 3:
                    for s in range(3):
                        sp.dma_start(W2[32 * s:32 * s + 32, :], b_gate_up[0]).then_inc(in_b, 16)
                    sp.dma_start(WR[:, :, :], w_router[0].rearrange("(k p) n -> p k n", p=P)).then_inc(in_r, 16)
                if u >= 5 and u < 8:
                    load_unit(u + 6)

            def load_piece(e, i, s):
                at, full, _ = place_of(i, s)
                dst = at if s < 8 else at.rearrange("p (k n) -> p k n", k=2)
                sp.dma_start(dst, piece_src(e, s)).then_inc(full, 16)

            def load_expert(e, i, pieces=range(PIECES), before=PLACES):
                for s in pieces:
                    sp.wait_ge(w_used, e * PIECES + (s + 1 - before))
                    load_piece(e, i, s)

            sp.wait_ge(v_pv, 2)
            sp.wait_ge(a_bo, NP2)
            for s in range(6, 10):
                load_piece(0, -1, s)
            for s in range(2):
                load_piece(1, 0, s)
            sp.wait_ge(m_half, 20)
            for s in range(2, 4):
                load_piece(1, 0, s)
            sp.wait_ge(m_mg, KC)
            for s in (0, 1, 10):
                load_piece(0, -1, s)
            sp.wait_ge(v_mg, KC)
            load_piece(0, -1, 11)
            sp.wait_ge(y_zero, 1)
            for hf in range(2):
                sp.dma_start(ysb[64 * hf:64 * hf + NE, :], b_down[0, :, hf * 512:(hf + 1) * 512]).then_inc(in_bd, 16)
            sp.wait_ge(m_wo, 4)
            for s in range(2, 6):
                load_piece(0, -1, s)
            for s in range(4, 7):
                load_piece(1, 0, s)
            sp.wait_ge(m_lr, TB)
            load_piece(1, 0, 7)
            load_expert(1, 0, range(8, PIECES), PLACES + OWN)
            load_expert(2, 1, range(0, 6), PLACES + OWN)
            load_expert(2, 1, range(6, PIECES))
            load_expert(3, 2)
            with sp.Fori(1, NE // 3) as j:
                for i in range(3):
                    load_expert(j * 3 + (1 + i), i)
            load_expert(NE - 1, 0)
            for b in range(TB):
                sp.wait_ge(v_out, b + 1)
                sp.dma_start(out[0, b * P:(b + 1) * P, :], XR[:, b, :]).then_inc(outs, 16)
            sp.wait_ge(outs, 32)

        @block.gpsimd
        def _(pool):
            nc.gpsimd.memset(mhalf[:, :], -0.5).then_inc(p_half, 1)
            pool.dma_start(qg[:, 0, :], q_norm_g.partition_broadcast(P)[:, 0, :]).then_inc(in_v, 16)
            pool.dma_start(qg[:, 1, :], k_norm_g.partition_broadcast(P)[:, 0, :]).then_inc(in_v, 16)
            pool.dma_start(br[:, :], b_router.partition_broadcast(P)[:, 0, :]).then_inc(in_v, 16)
            nc.gpsimd.memset(ONEB[:, :], 1.0).then_inc(bias_ok, 1)
            nc.gpsimd.memset(zero[:, :], 0.0).then_inc(z_ok, 1)


            def inverse_root(n, count):
                pool.wait_ge(v_ms, count)
                nc.gpsimd.tensor_tensor(sm[:, 40:40 + n], sm[:, 20:20 + n], mhalf[:, 0:n], ALU.pow).then_inc(p_rt, 1)

            pool.wait_ge(p_half, 1)
            inverse_root(2, 1)
            inverse_root(18, 2)
            pool.wait_ge(in_b, 48)
            n = 0
            for j in range(3):
                for q in range(j, 3):
                    r = slice(32 * q, 32 * q + 32)
                    if j:
                        nc.gpsimd.tensor_tensor(W2[r, :], W2[r, :], bias3[r, :], ALU.subtract).then_inc(g_chain, 1)
                        n += 1
                        pool.wait_ge(g_chain, n)
                    ins = nc.gpsimd.tensor_copy(bias3[r, :], W2[r, :])
                    if q == 2 and j == 2:
                        ins.then_inc(bias_ok, 1)
                    else:
                        ins.then_inc(g_chain, 1)
                        n += 1
                        pool.wait_ge(g_chain, n)
            inverse_root(1, 3)
            inverse_root(1, 4)

        @block.tensor
        def _(pe):
            mm, tr = nc.tensor.matmul, nc.tensor.transpose
            nhalf = [0]

            def half_bank():
                h = nhalf[0]
                if h >= 2:
                    pe.wait_ge(a_half, h - 1)
                return Pp[:, h % 2, :]

            def close_half(ins):
                ins.then_inc(m_half, 1)
                nhalf[0] += 1

            def token_half(u, b, n):
                if b == 0:
                    pe.wait_ge(unit_in[u], 16 * len(units[u]))
                bank = half_bank()
                for k in range(KC):
                    last = mm(bank[:, 0:n], XT[:, k, b * P:(b + 1) * P], uview(u, n)[:, k, :],
                              start=k == 0, stop=k == KC - 1)
                close_half(last)

            def column_half(u, hf):
                if hf == 0:
                    pe.wait_ge(unit_in[u], 16)
                bank = half_bank()
                for t in range(2):
                    for k in range(KC):
                        c = (2 * hf + t) * P
                        last = mm(bank[:, t * SEQ:(t + 1) * SEQ], uview(u)[:, k, c:c + P], XT[:, k, :],
                                  start=k == 0, stop=k == KC - 1)
                close_half(last)

            pe.wait_ge(in_id, 16)
            pe.wait_ge(in_g, 32)
            tr(Bp[:, 1, 0:2 * KC], gst[:, :], ident[0:2 * KC, 0:2 * KC]).then_inc(m_gn, 1)
            pe.wait_ge(v_xr, 2)
            for k in range(KC):
                for b in range(TB):
                    last = tr(Ap[:, k // 2, (k % 2) * SEQ + b * P:(k % 2) * SEQ + (b + 1) * P],
                              XR[:, b, k * P:(k + 1) * P], ident)
                if k % 4 == 3:
                    last.then_inc(m_xt, 1)
            pe.wait_ge(a_xt, 4)
            pe.wait_ge(v_xt, 4)
            for u, n in ((0, 512), (1, 200), (2, 512)):
                for b in range(TB):
                    token_half(u, b, n)

            def query_key_transposes(q0, kbank):
                for b in range(TB):
                    for j in range(NP2):
                        tr(Ap[:, q0 + j // 2, (j % 2) * SEQ + b * P:(j % 2) * SEQ + (b + 1) * P],
                           TM[:, b, (QI if q0 == 0 else QA) + j * P:][:, 0:P], ident)
                    last = tr(kbank[:, b * P:(b + 1) * P], KD[:, b, 0:P] if q0 == 0 else KD[:, b, P:2 * P], ident)
                return last

            pe.wait_ge(v_roti, 1)
            query_key_transposes(0, Ap[:, 2, :]).then_inc(m_ti, 1)

            def head_products(qT, kT, b, base, nk):
                for j in range(NP2):
                    for r in range(2):
                        h = slice(64 * r, 64 * r + 64)
                        if nk == SEQ:
                            dst = Ap[:, 2 * r + j // 2, (j % 2) * SEQ:(j % 2 + 1) * SEQ]
                        else:
                            dst = Ap[:, base + r, j * P:(j + 1) * P]
                        last = mm(dst, qT[h, j, b * P:(b + 1) * P], kT[h, 0:nk], start=True, stop=True)
                return last

            def b_logits(p):
                if p >= 1:
                    pe.wait_ge(a_bo, p)
                for r in range(2):
                    h = slice(64 * r, 64 * r + 64)
                    mm(Bp[:, r, 0:SEQ], KBT[h, p, 0:P], QBT[h, p, :], start=True, stop=False, skip_group_check=True)
                for r in range(2):
                    h = slice(64 * r, 64 * r + 64)
                    last = mm(Bp[:, r, SEQ:384], KBT[h, p, P:SEQ], QBT[h, p, P:SEQ], start=False, stop=False,
                              skip_group_check=True)
                last.then_inc(m_bz, 1)

            def b_sums(p):
                pe.wait_ge(v_bs, p + 1)
                for r in range(2):
                    mm(Bp[:, r, 0:384], lneg, SPt[:, r, :], start=False, stop=False, skip_group_check=True)
                    last = mm(Bp[:, r, P:SEQ], oneg, SPt[:, r, SEQ:384], start=False, stop=True,
                              skip_group_check=True)
                last.then_inc(m_bc, 1)

            def b_values(p):
                pe.wait_ge(a_bp, p + 1)
                for r in range(2):
                    c = slice((2 * p + r) * HD, (2 * p + r + 1) * HD)
                    mm(Bp[64 * r:64 * r + 64, 0, 0:SEQ], VBt[:, 0, c], ET[:, r, 0:SEQ], start=True, stop=False,
                       skip_group_check=True)
                for r in range(2):
                    c = slice((2 * p + r) * HD, (2 * p + r + 1) * HD)
                    last = mm(Bp[64 * r:64 * r + 64, 0, P:SEQ], VBt[:, 1, c], ET[:, r, SEQ:384], start=False,
                              stop=True, skip_group_check=True)
                last.then_inc(m_bv, 1)

            def turn_probabilities(b, count):
                pe.wait_ge(v_pr, count)
                if b == 0:
                    pe.wait_ge(v_pv, 1)
                nk = P * (b + 1)
                for r in range(2):
                    for kb in range(b + 1):
                        for j in range(NP2):
                            c = (r * NP2 + j) * nk + kb * P
                            last = tr(Ap[:, r * (b + 1) + kb, j * P:(j + 1) * P], W1[:, c:c + P], ident)
                last.then_inc(m_pt, 1)

            def a_values(b, bank, count):
                pe.wait_ge(v_pt, count)
                for kb in range(b + 1):
                    for r in range(2):
                        c = (r * (b + 1) + kb) * 512
                        last = mm(Ap[64 * r:64 * r + 64, bank, :], TM[:, kb, VA:VA + HD], W2[:, c:c + 512],
                                  start=kb == 0, stop=kb == b, skip_group_check=True)
                last.then_inc(m_pv, 1)

            column_half(3, 0)
            pe.wait_ge(v_ti, 1)
            head_products(QIT, KIT, 1, 0, SEQ).then_inc(m_sc, 1)
            column_half(3, 1)
            column_half(4, 0)
            pe.wait_ge(a_relu, 1)
            head_products(QIT, KIT, 0, 0, P).then_inc(m_sc, 1)
            pe.wait_ge(v_rota, 1)
            query_key_transposes(2, Bp[:, 0, :]).then_inc(m_ta, 1)
            column_half(4, 1)
            token_half(5, 0, 512)
            pe.wait_ge(a_half, 10)
            pe.wait_ge(v_ta, 1)
            b_logits(0)
            pe.wait_ge(a_relu, 2)
            head_products(QAT, KAT, 1, 0, SEQ).then_inc(m_lg, 1)
            token_half(5, 1, 512)
            b_sums(0)
            column_half(6, 0)
            pe.wait_ge(a_half, 12)
            b_values(0)
            b_logits(1)
            column_half(6, 1)
            b_sums(1)
            column_half(7, 0)
            b_values(1)
            b_logits(2)
            turn_probabilities(1, 1)
            column_half(7, 1)
            b_sums(2)
            a_values(1, 0, 1)
            head_products(QAT, KAT, 0, 2, P).then_inc(m_lg, 1)
            column_half(8, 0)
            b_values(2)
            b_logits(3)
            column_half(8, 1)
            b_sums(3)
            turn_probabilities(0, 2)
            column_half(9, 0)
            b_values(3)
            a_values(0, 2, 2)
            column_half(9, 1)

            pe.wait_ge(v_pv, 2)
            pe.wait_ge(a_bo, NP2)
            for c in range(KC):
                if c >= 2:
                    pe.wait_ge(v_mg, c - 1)
                else:
                    pe.wait_ge(a_half, nhalf[0] - 1 + c)
                for ab, (u, o) in enumerate(((10, OAT), (11, OBT))):
                    pe.wait_ge(unit_in[u], 16)
                    for j in range(NP2):
                        last = mm(Pp[:, c % 2, ab * SEQ:(ab + 1) * SEQ], urows(u)[:, j, c * P:(c + 1) * P],
                                  o[:, j, :], start=j == 0, stop=j == NP2 - 1)
                last.then_inc(m_mg, 1)
            def out_projection(b, hf):
                for c in range(KC):
                    if b == 0 and hf == 0:
                        pe.wait_ge(v_mg, c + 1)
                        if c % 4 == 0:
                            pe.wait_ge(unit_in[12 + c // 4], 16)
                    last = mm(Ap[:, 2 * b + hf, :], XT[:, c, b * P:(b + 1) * P],
                              urows(12 + c // 4)[:, c % 4, hf * 512:(hf + 1) * 512], start=c == 0, stop=c == KC - 1)
                last.then_inc(m_wo, 1)

            def turn_h(b):
                for i in range(2):
                    pe.wait_ge(v_xr, 3 + 2 * b + i)
                    for k in range(4 * i, 4 * i + 4):
                        last = tr(Ap[:, 2 * b + i, (k % 4) * P:(k % 4 + 1) * P], XR[:, b, k * P:(k + 1) * P], ident)
                    last.then_inc(m_xt, 1)

            def router_products(b):
                for k in range(KC):
                    if k == 0:
                        pe.wait_ge(v_xt, 5 + b)
                    if k == 4:
                        pe.wait_ge(a_xt, 8 + 4 * b)
                    last = mm(Pp[:, 0, b * NE:(b + 1) * NE], XT[:, k, b * P:(b + 1) * P], WR[:, k, :],
                              start=k == 0, stop=k == KC - 1)
                last.then_inc(m_lr, 1)

            pe.wait_ge(in_r, 16)
            out_projection(0, 0)
            out_projection(0, 1)
            out_projection(1, 0)
            turn_h(0)
            out_projection(1, 1)
            router_products(0)
            turn_h(1)
            router_products(1)
            pe.wait_ge(z_ok, 1)
            for bank in range(4):
                mm(Ap[:, bank, :], zero[:, 0:P], zero[:, P:], start=True, stop=False, skip_group_check=True)
            pe.wait_ge(v_as, TB)
            mm(Pp[:, 1, 0:NE], strict, AS[:, 0, :], start=True, stop=True)
            mm(Pp[:, 1, NE:2 * NE], ones, AS[:, 0, :], start=True, stop=False)
            mm(Pp[:, 1, NE:2 * NE], strict, AS[:, 1, :], start=False, stop=True)
            mm(Pp[:, 1, 2 * NE:3 * NE], ones, AS[:, 0, :], start=True, stop=False)
            mm(Pp[:, 1, 2 * NE:3 * NE], ones, AS[:, 1, :], start=False, stop=True).then_inc(m_rk, 1)
            pe.wait_ge(v_gp, TB)
            for b in range(TB):
                last = tr(Bp[:, 0, b * P:(b + 1) * P], GPAD[:, b, :], ident)
            last.then_inc(m_g, 1)
            def scatter():
                for b in range(TB):
                    for hf in range(2):
                        h = slice(64 * hf, 64 * hf + 64)
                        last = mm(Ap[:, 2 * b + hf, :], GT[h, b * P:(b + 1) * P], ysb[h, :],
                                  start=False, stop=False, skip_group_check=True)
                return last

            count = pe.alloc_register("pe_count")

            def expert_block(n, j, i, release, next_count=None):
                def piece(s):
                    at, full, fills = place_of(i, s)
                    pe.wait_ge(full, j * 32 + fills * 16)
                    return at

                pe.wait_ge(d_oh, n)
                for k in range(KC):
                    for b in range(TB):
                        last = mm(Tps[:, k * SLOTS:(k + 1) * SLOTS], XR[:, b, k * P:(k + 1) * P], OH[:, b, :],
                                  start=b == 0, stop=b == 1)
                last.then_inc(m_ga, 1)
                pe.wait_ge(d_xt, n)
                pe.wait_ge(a_gt, n)
                for q in range(4):
                    mm((Gps, Ups)[q // 2][64 * (q % 2):64 * (q % 2) + 64, :], SELE[:, :],
                       bias3[:, q * 512:(q + 1) * 512], start=True, stop=False, skip_group_check=True)
                for k in range(KC):
                    w = piece(k)
                    for q in range(4):
                        last = mm((Gps, Ups)[q // 2][64 * (q % 2):64 * (q % 2) + 64, :], xT[:, k, :],
                                  w[:, q * 512:(q + 1) * 512], start=False, stop=k == KC - 1, skip_group_check=True)
                    if release and k < KC - 1:
                        last.then_inc(w_used, 1)
                last.then_inc(m_gu, 1)
                pe.wait_ge(a_y, n)
                last = scatter()
                if release:
                    last.then_inc(w_used, 1)
                if next_count is not None:
                    pe.reg_load(count, next_count)
                pe.wait_ge(d_act, n)
                for c in range(4):
                    last = tr(Yps[:, c * P:(c + 1) * P], actb[:, c * P:(c + 1) * P], ident)
                last.then_inc(m_ht, 1)
                pe.wait_ge(d_ht, n)
                for s in range(4):
                    w = piece(8 + s)
                    for half in range(2):
                        k = 2 * s + half
                        for hf in range(2):
                            last = mm(Yps[64 * hf:64 * hf + 64, :], hT[:, k % 4, k // 4, :],
                                      w[:, half * 1024 + hf * 512:][:, 0:512], start=k == 0, stop=k == KC - 1,
                                      skip_group_check=True)
                    if release and s < 3:
                        last.then_inc(w_used, 1)
                last.then_inc(m_y, 1)
                first = tr(Gps[:, 0:P], PG[:, 0, :], ident)
                if release:
                    first.then_inc(w_used, 1)
                tr(Gps[:, P:SEQ], PG[:, 1, :], ident).then_inc(m_gt, 1)

            pe.wait_ge(bias_ok, 2)
            pe.wait_ge(v_rk, 1)
            extra = pe.alloc_register("pe_extra")
            pe.reg_mov(extra, 1)
            pe.reg_load(count, CNT[0:1, 0:1])
            pe.sem_inc(m_gt, 1)

            def expert(j, i):
                e = j * 3 + (1 + i)
                with pe.If(pe.snap(count) > SLOTS):
                    with pe.Fori(1, SEQ // SLOTS) as block_no:
                        expert_block(pe.snap(extra) + e + (block_no - 1), j, i, False)
                    pe.reg_add(extra, extra, SEQ // SLOTS - 1)
                expert_block(pe.snap(extra) + e, j, i, True, CNT[0:1, bass.ds(e + 1, 1)])

            pe.wait_ge(a_g, 1)
            pe.wait_ge(in_bd, 32)
            expert(0, -1)
            with pe.Fori(0, NE // 3) as j:
                for i in range(3):
                    expert(j, i)
            expert(NE // 3, 0)
            pe.wait_ge(a_y, pe.snap(extra) + NE)
            pe.wait_ge(a_gt, pe.snap(extra) + NE)
            for b in range(TB):
                for hf in range(2):
                    h = slice(64 * hf, 64 * hf + 64)
                    last = mm(Ap[:, 2 * b + hf, :], GT[h, b * P:(b + 1) * P], ysb[h, :],
                              start=False, stop=True, skip_group_check=True)
                last.then_inc(m_end, 1)

        @block.vector
        def _(dve):
            V = nc.vector
            chain = [0]

            def link(ins):
                chain[0] += 1
                ins.then_inc(v_chain, 1)
                dve.wait_ge(v_chain, chain[0])

            def rsqrt(ss, n, width, count):
                v, y, t = (sm[:, i:i + n] for i in (20, 40, 60))
                V.tensor_scalar(v, ss, 1.0 / width, EPS, ALU.mult, ALU.add).then_inc(v_ms, 1)
                dve.wait_ge(p_rt, count)
                link(V.tensor_tensor(t, y, y, ALU.mult))
                link(V.tensor_tensor(t, t, v, ALU.mult))
                link(V.tensor_scalar(t, t, -0.5, 1.5, ALU.mult, ALU.add))
                link(V.tensor_tensor(y, y, t, ALU.mult))
                return y

            def rotate(view, nheads):
                tmp = RT.rearrange("p a t -> p (a t)")[:, 0:2 * TB * nheads * ROT].rearrange(
                    "p (z b h r) -> p z b h r", z=2, b=TB, h=nheads)
                for b in range(TB):
                    cb = cosd[:, b:b + 1, :].to_broadcast([P, nheads, ROT])
                    nb = sinn[:, b:b + 1, :].to_broadcast([P, nheads, RH])
                    pb = sinp[:, b:b + 1, :].to_broadcast([P, nheads, RH])
                    V.tensor_tensor(tmp[:, 0, b], view[:, b, :, 0:ROT], cb, ALU.mult)
                    V.tensor_tensor(tmp[:, 1, b, :, 0:RH], view[:, b, :, RH:ROT], nb, ALU.mult)
                    link(V.tensor_tensor(tmp[:, 1, b, :, RH:ROT], view[:, b, :, 0:RH], pb, ALU.mult))
                for b in range(TB):
                    last = V.tensor_tensor(view[:, b, :, 0:ROT], tmp[:, 0, b], tmp[:, 1, b], ALU.add)
                return last

            dve.wait_ge(in_x[1], 16)
            link(V.tensor_tensor_reduce(XR[:, 1, :], X[:, 1, :], X[:, 1, :], 1.0, 0.0, ALU.mult, ALU.add, sm[:, 1:2]))
            dve.wait_ge(a_sq, 1)
            y = rsqrt(sm[:, 0:2], 2, D, 1)
            for b in range(TB):
                V.tensor_scalar(XR[:, b, :], X[:, b, :], y[:, b:b + 1], None, ALU.mult).then_inc(v_xr, 1)

            dve.wait_ge(a_gn, 1)
            dve.wait_ge(m_xt, 2)
            for k in range(4, KC):
                V.tensor_scalar(XT[:, k, :], Ap[:, k // 2, (k % 2) * SEQ:(k % 2 + 1) * SEQ], g_mix[:, k:k + 1], None,
                                ALU.mult).then_inc(v_xt, 1)

            dve.wait_ge(a_half, 4)
            dve.wait_ge(in_c, 16)
            qi9 = TM[:, :, QI:QI + 9 * HD].rearrange("p b (h d) -> p b h d", h=9)
            link(rotate(qi9, 9))
            for b in range(TB):
                last = V.tensor_copy(KD[:, b, 0:P].rearrange("p (r d) -> p r d", r=2),
                                     TM[:, b:b + 1, KI:KI + HD].to_broadcast([P, 2, HD]))
            wis = sm[:, 100:116].rearrange("p (b h) -> p b h", b=TB)
            link(last)
            link(V.tensor_scalar(wis, TM[:, :, WI:WI + NH], NH ** -0.5, None, ALU.mult))
            dve.sem_inc(v_roti, 1)

            dve.wait_ge(m_ti, 1)
            V.tensor_copy(QIT, Ap[:, 0:2, :].rearrange("p a (j t) -> p (a j) t", j=2))
            V.tensor_copy(KIT, Ap[:, 2, 0:SEQ]).then_inc(v_ti, 1)
            dve.wait_ge(a_half, 6)
            dve.wait_ge(in_v, 48)
            link(V.tensor_scalar(qg[:, 0, :], qg[:, 0, :], HSCALE, None, ALU.mult))
            for b in range(TB):
                qk = TM[:, b, 0:9 * HD]
                link(V.tensor_tensor(MB[:, :, :].rearrange("p b s -> p (b s)")[:, 0:512], qk[:, 0:512], qk[:, 0:512],
                                     ALU.mult))
                V.tensor_reduce(sm[:, 120 + 9 * b:128 + 9 * b],
                                MB[:, :, :].rearrange("p b s -> p (b s)").rearrange("p (h d) -> p h d", h=NH),
                                AX_X, ALU.add)
                link(V.tensor_tensor(SC[:, 0, 0:HD], qk[:, 512:576], qk[:, 512:576], ALU.mult))
                link(V.tensor_reduce(sm[:, 128 + 9 * b:129 + 9 * b], SC[:, 0, 0:HD], AX_X, ALU.add))
            y = rsqrt(sm[:, 120:138], 18, HD, 2)
            for b in range(TB):
                q9 = TM[:, b, 0:9 * HD].rearrange("p (h d) -> p h d", h=9)
                link(V.tensor_tensor(q9, q9, y[:, 9 * b:9 * b + 9].unsqueeze(2).to_broadcast([P, 9, HD]), ALU.mult))
                V.tensor_tensor(q9[:, 0:8, :], q9[:, 0:8, :], qg[:, 0:1, :].to_broadcast([P, 8, HD]), ALU.mult)
                link(V.tensor_tensor(q9[:, 8:9, :], q9[:, 8:9, :], qg[:, 1:2, :], ALU.mult))
            link(rotate(TM[:, :, 0:9 * HD].rearrange("p b (h d) -> p b h d", h=9), 9))
            for b in range(TB):
                last = V.tensor_copy(KD[:, b, P:2 * P].rearrange("p (r d) -> p r d", r=2),
                                     TM[:, b:b + 1, KA:KA + HD].to_broadcast([P, 2, HD]))
            last.then_inc(v_rota, 1)

            def index_scores(b, nk, count):
                dve.wait_ge(a_relu, count)
                prev = adm[:, b, 0:nk]
                for j in range(NP2):
                    for r in range(2):
                        hh = r * 4 + j
                        link(V.scalar_tensor_tensor(out=SC[:, b, 0:nk], in0=W1[:, hh * nk:(hh + 1) * nk],
                                                    scalar=wis[:, b, 2 * j + r:2 * j + r + 1], in1=prev,
                                                    op0=ALU.mult, op1=ALU.add))
                        prev = SC[:, b, 0:nk]
                dve.sem_inc(v_sum, 1)

            def select_keys(b, nk):
                top = sm[:, 140:148]
                for _ in range(SEL // 8):
                    link(V.max(top, SC[:, b, 0:nk]))
                    link(V.match_replace(SC[:, b, 0:nk], top, SC[:, b, 0:nk], TAKEN))
                link(V.tensor_scalar(MB[:, b, 0:nk], SC[:, b, 0:nk], -2e38, NEG, ALU.is_gt, ALU.mult))

            def mask_logits(b, nk, src, count):
                dve.wait_ge(m_lg, count)
                L = W1[:, 0:NH * nk].rearrange("p (h s) -> p h s", h=NH)
                link(V.tensor_tensor(L, src, MB[:, b:b + 1, 0:nk].to_broadcast([P, NH, nk]), ALU.add))
                link(V.tensor_reduce(sm[:, 0:8], L, AX_X, ALU.max))
                V.tensor_scalar(sm[:, 8:16], sm[:, 0:8], -1.0, None, ALU.mult).then_inc(v_lg, 1)

            def normalise(nk, count):
                dve.wait_ge(a_ex, NH * count)
                link(V.reciprocal(sm[:, 148:156], sm[:, 80:88]))
                L = W1[:, 0:NH * nk].rearrange("p (h s) -> p h s", h=NH)
                V.tensor_tensor(L, L, sm[:, 148:156].unsqueeze(2).to_broadcast([P, NH, nk]), ALU.mult)\
                    .then_inc(v_pr, 1)

            def b_softplus(p):
                dve.wait_ge(a_bl, p + 1)
                link(V.scalar_tensor_tensor(out=SPt, in0=Bp[:, :, 0:384], scalar=0.0, in1=ET, op0=ALU.max, op1=ALU.add))
                for r in range(2):
                    d = SPt[:, r, :].rearrange("p (g q) -> p g q", g=3)[:, 0:3:2, :]
                    last = V.tensor_tensor(d, d, cst[:, C_STRICT:C_STRICT + P].unsqueeze(1).to_broadcast([P, 2, P]),
                                           ALU.mult)
                last.then_inc(v_bs, 1)

            def b_argument(p):
                dve.wait_ge(m_bc, p + 1)
                V.scalar_tensor_tensor(out=NT, in0=Bp[:, :, 0:384], scalar=0.0,
                                       in1=causal.unsqueeze(1).to_broadcast([P, 2, 384]),
                                       op0=ALU.min, op1=ALU.add).then_inc(v_ba, 1)

            def out_of_bank(sem_, count, dst, src, done):
                dve.wait_ge(sem_, count)
                V.tensor_copy(dst, src).then_inc(done, 1)

            index_scores(1, SEQ, 1)
            dve.wait_ge(m_ta, 1)
            V.tensor_copy(QAT[:, :, :], Ap[:, 2:4, :].rearrange("p a (j t) -> p (a j) t", j=2))
            V.tensor_copy(KAT[:, :], Bp[:, 0, 0:SEQ]).then_inc(v_ta, 1)
            select_keys(1, SEQ)
            index_scores(0, P, 2)
            b_softplus(0)
            mask_logits(1, SEQ, Ap[:, :, :].rearrange("p a (j s) -> p (a j) s", j=2), 1)
            b_argument(0)
            select_keys(0, P)
            b_softplus(1)
            normalise(SEQ, 1)
            b_argument(1)
            dve.wait_ge(bias_ok, 2)
            out_of_bank(m_pt, 1, W2, Ap[:, :, :].rearrange("p a n -> p (a n)"), v_pt)
            b_softplus(2)
            b_argument(2)
            out_of_bank(m_pv, 1, OAT[:, :, P:SEQ], Ap[:, 0, :].rearrange("p (j q) -> p j q", j=NP2), v_pv)
            mask_logits(0, P, Ap[:, 2:4, :].rearrange("p a (j s) -> p (a j) s", j=NP2), 2)
            b_softplus(3)
            normalise(P, 2)
            b_argument(3)
            out_of_bank(m_pt, 2, W2[:, 0:1024], Ap[:, 0:2, :].rearrange("p a n -> p (a n)"), v_pt)
            out_of_bank(m_pv, 2, OAT[:, :, 0:P], Ap[:, 2, :].rearrange("p (j q) -> p j q", j=NP2), v_pv)

            for c in range(KC):
                dve.wait_ge(m_mg, c + 1)
                dve.wait_ge(a_sig, c // 2 + 1)
                gc = G[:, c, :, :].rearrange("p r t -> p (r t)")
                link(V.tensor_tensor(gc, gc, Pp[:, c % 2, :], ALU.mult))
                V.tensor_tensor(XT[:, c, :], G[:, c, 0, :], G[:, c, 1, :], ALU.add).then_inc(v_mg, 1)
            dve.wait_ge(v_mg, KC)
            V.memset(GPAD, 0.0)
            V.memset(ysb, 0.0).then_inc(y_zero, 1)

            def add_residual(b, hf):
                dve.wait_ge(m_wo, 2 * b + hf + 1)
                h = X[:, b, hf * 512:(hf + 1) * 512]
                link(V.tensor_tensor(h, h, Ap[:, 2 * b + hf, :], ALU.add))
                link(V.tensor_tensor_reduce(XR[:, b, hf * 512:(hf + 1) * 512], h, h, 1.0, 0.0, ALU.mult, ALU.add,
                                            sm[:, hf:hf + 1]))

            def norm_h(b):
                link(V.tensor_tensor(sm[:, 2:3], sm[:, 0:1], sm[:, 1:2], ALU.add))
                y = rsqrt(sm[:, 2:3], 1, D, 3 + b)
                for hf in range(2):
                    h = slice(hf * 512, (hf + 1) * 512)
                    V.tensor_scalar(XR[:, b, h], X[:, b, h], y, None, ALU.mult).then_inc(v_xr, 1)

            def gain_h(b):
                dve.wait_ge(m_xt, 3 + 2 * b)
                V.tensor_tensor(XT[:, 0:4, b * P:(b + 1) * P], Ap[:, 2 * b, :].rearrange("p (k t) -> p k t", k=4),
                                g_ffn[:, 0:4].unsqueeze(2).to_broadcast([P, 4, P]), ALU.mult).then_inc(v_xt, 1)

            def route(b):
                dve.wait_ge(m_lr, b + 1)
                link(V.tensor_tensor(LGT[:, b, :], Pp[:, 0, b * NE:(b + 1) * NE], br[:, :], ALU.add))
                link(V.max(M8[:, b, :], LGT[:, b, :]))
                V.tensor_scalar(G4[:, b, :], M8[:, b, 0:TOPK], M8[:, b, 0:1], None, ALU.subtract).then_inc(v_tk, 1)
                link(V.max_index(I8[:, b, :], M8[:, b, :], LGT[:, b, :]))
                link(V.tensor_copy(IXF[:, b, :], I8[:, b, :]))
                link(V.tensor_tensor(EQ[:, b], e32.unsqueeze(1).to_broadcast([P, TOPK, NE]),
                                     IXF[:, b, 0:TOPK].unsqueeze(2).to_broadcast([P, TOPK, NE]), ALU.is_equal))
                V.tensor_reduce(AS[:, b, :], EQ[:, b].rearrange("p k e -> p e k"), AX_X, ALU.add).then_inc(v_as, 1)
                dve.wait_ge(a_ge, b + 1)
                link(V.tensor_reduce(sm[:, 4 + b:5 + b], G4[:, b, :], AX_X, ALU.add))
                link(V.reciprocal(sm[:, 6 + b:7 + b], sm[:, 4 + b:5 + b]))
                link(V.tensor_tensor(GQ[:, b], EQ[:, b], G4[:, b, :].unsqueeze(2).to_broadcast([P, TOPK, NE]),
                                     ALU.mult))
                link(V.tensor_reduce(GPAD[:, b, 0:NE], GQ[:, b].rearrange("p k e -> p e k"), AX_X, ALU.add))
                link(V.tensor_scalar(GPAD[:, b, 0:NE], GPAD[:, b, 0:NE], sm[:, 6 + b:7 + b], None, ALU.mult))
                V.tensor_copy(GPAD[:, b, 64:64 + NE], GPAD[:, b, 0:NE])
                V.tensor_copy(GE[:, :, b], GPAD[:, b, 0:NE]).then_inc(v_gp, 1)

            add_residual(0, 0)
            add_residual(0, 1)
            norm_h(0)
            add_residual(1, 0)
            gain_h(0)
            add_residual(1, 1)
            norm_h(1)
            route(0)
            gain_h(1)
            route(1)
            dve.wait_ge(m_rk, 1)
            link(V.scalar_tensor_tensor(out=LGT, in0=Pp[:, 1, 0:TB * NE].rearrange("p (b e) -> p b e", b=TB),
                                        scalar=1.0, in1=AS, op0=ALU.add, op1=ALU.mult))
            link(V.tensor_scalar(RK.rearrange("p e b -> p b e"), LGT, -1.0, None, ALU.add))
            V.memset(CNT[:, NE:NE + 1], 0)
            V.tensor_copy(CNT[:, 0:NE], Pp[:, 1, 2 * NE:3 * NE]).then_inc(v_rk, 1)

            def expert_block(n, e, offset):
                if offset is None:
                    V.tensor_copy(rkc, RK[:, bass.ds(e, 1), :].rearrange("p e b -> p (e b)"))
                else:
                    V.tensor_scalar(rkc, RK[:, bass.ds(e, 1), :].rearrange("p e b -> p (e b)"),
                                    off[:, bass.ds(offset, 1)], None, ALU.subtract)
                V.tensor_scalar(SELE[:, :], ONEB[:, :], eye3[:, bass.ds(e, 1)], None, ALU.mult)
                V.tensor_copy(gtc, GE[:, bass.ds(e, 1), :].rearrange("p e b -> p (e b)")).then_inc(d_loc, 1)
                dve.wait_ge(d_loc, n * 4 - 3)
                for b in range(TB):
                    last = V.tensor_scalar(OH[:, b, :], slots[:, 0:SLOTS], rkc[:, b:b + 1], None, ALU.is_equal)
                last.then_inc(d_oh, 1)
                dve.wait_ge(m_ga, n)
                V.tensor_tensor(xT, Tps.rearrange("p (k s) -> p k s", k=KC),
                                g_ffn[:, :].unsqueeze(2).to_broadcast([P, KC, SLOTS]), ALU.mult).then_inc(d_xt, 1)
                dve.wait_ge(m_gt, n)
                for b in range(TB):
                    V.tensor_scalar(PG[:, b, :], slots, rkc[:, b:b + 1], gtc[:, b:b + 1], ALU.is_equal, ALU.mult)
                dve.wait_ge(m_gu, n)
                V.tensor_scalar(gm, Gps, LIMIT, None, ALU.min).then_inc(d_gm, 1)
                V.tensor_scalar(u1, Ups, LIMIT, -LIMIT, ALU.min, ALU.max).then_inc(d_loc, 1)
                dve.wait_ge(d_loc, n * 4 - 2)
                V.scalar_tensor_tensor(out=tu, in0=u1, scalar=1.0, in1=gm, op0=ALU.add, op1=ALU.mult)\
                    .then_inc(d_loc, 1)
                dve.wait_ge(d_loc, n * 4 - 1)
                dve.wait_ge(a_sg, n)
                V.tensor_tensor(actb, tu, sg, ALU.mult).then_inc(d_act, 1)
                dve.wait_ge(m_ht, n)
                V.tensor_copy(hTf, Yps).then_inc(d_ht, 1)
                dve.sem_inc(d_loc, 1)

            dve.wait_ge(v_rk, 1)
            extra = dve.alloc_register("dve_extra")
            dve.reg_mov(extra, 1)
            with dve.Fori(0, NE) as e:
                count = dve.value_load(CNT[0:1, bass.ds(e, 1)], min_val=0, max_val=SEQ)
                with dve.If(count > SLOTS):
                    with dve.Fori(1, SEQ // SLOTS) as j:
                        expert_block(dve.snap(extra) + e + (j - 1), e, j)
                    dve.reg_add(extra, extra, SEQ // SLOTS - 1)
                expert_block(dve.snap(extra) + e, e, None)
            for b in range(TB):
                dve.wait_ge(m_end, b + 1)
                V.tensor_tensor(XR[:, b, :], X[:, b, :], Ap[:, 2 * b:2 * b + 2, :].rearrange("p a n -> p (a n)"),
                                ALU.add).then_inc(v_out, 1)

        @block.scalar
        def _(act):
            A = nc.scalar.activation

            nh = [0]

            def evacuate(*parts):
                act.wait_ge(m_half, nh[0] + 1)
                bank = Pp[:, nh[0] % 2, :]
                for i, (dst, a, n, scale) in enumerate(parts):
                    src = bank[:, a:a + n]
                    if len(dst.shape) == 3:
                        src = src.rearrange("p (j t) -> p j t", t=dst.shape[2])
                    ins = A(dst, src, ACT.Copy, scale=scale)
                ins.then_inc(a_half, 1)
                nh[0] += 1

            act.dma_start(gst[0:KC, :], norm_mix_g[0].rearrange("(k p) -> k p", p=P)).then_inc(in_g, 16)
            act.dma_start(gst[KC:2 * KC, :], norm_ffn_g[0].rearrange("(k p) -> k p", p=P)).then_inc(in_g, 16)
            act.wait_ge(in_x[0], 16)
            A(XR[:, 0, :], X[:, 0, :], ACT.Square, accum_out=sm[:, 0:1]).then_inc(a_sq, 1)
            act.wait_ge(m_gn, 1)
            A(gains[:, :], Bp[:, 1, 0:2 * KC], ACT.Copy).then_inc(a_gn, 1)
            act.wait_ge(a_gn, 1)
            act.wait_ge(m_xt, 1)
            for k in range(4):
                A(XT[:, k, :], Ap[:, k // 2, (k % 2) * SEQ:(k % 2 + 1) * SEQ], ACT.Copy,
                  scale=g_mix[:, k:k + 1]).then_inc(a_xt, 1)
            for b in range(TB):
                evacuate((TM[:, b, QI:QI + 512], 0, 512, HSCALE))
            for b in range(TB):
                evacuate((TM[:, b, KI:KI + 72], 0, 72, 1.0), (TM[:, b, KA:KA + 128], 72, 128, 1.0))
            for b in range(TB):
                evacuate((TM[:, b, QA:QA + 512], 0, 512, 1.0))

            def relu(b, n, count):
                act.wait_ge(m_sc, count)
                A(W1[:, 0:n], Ap[:, 0:n // 512, :].rearrange("p a n -> p (a n)"), ACT.Relu).then_inc(a_relu, 1)

            def b_log(p):
                act.wait_ge(m_bz, p + 1)
                A(ET, Bp[:, :, 0:384], ACT.Abs).then_inc(a_chain, 1)
                act.wait_ge(a_chain, 2 * p + 1)
                A(ET, ET, ACT.Exp, scale=-1.0).then_inc(a_chain, 1)
                act.wait_ge(a_chain, 2 * p + 2)
                A(ET, ET, ACT.Ln, bias=1.0).then_inc(a_bl, 1)

            def b_exp(p):
                act.wait_ge(v_ba, p + 1)
                A(ET, NT, ACT.Exp).then_inc(a_bp, 1)

            def b_out(p):
                act.wait_ge(m_bv, p + 1)
                A(OBT[:, p, :], Bp[:, 0, 0:SEQ], ACT.Copy).then_inc(a_bo, 1)

            def a_exp(nk, count):
                act.wait_ge(v_lg, count)
                for h in range(NH):
                    A(W1[:, h * nk:(h + 1) * nk], W1[:, h * nk:(h + 1) * nk], ACT.Exp, bias=sm[:, 8 + h:9 + h],
                      accum_out=sm[:, 80 + h:81 + h]).then_inc(a_ex, 1)

            def gate_half(u, hf):
                ab, c = (u - 6) // 2, 4 * ((u - 6) % 2) + 2 * hf
                evacuate((G[:, c:c + 2, ab, :], 0, 512, 1.0))

            evacuate((QBT[:, 0:2, :], 0, 512, HSCALE))
            relu(1, 2048, 1)
            evacuate((QBT[:, 2:4, :], 0, 512, HSCALE))
            evacuate((KBT[:, 0:2, :], 0, 512, 1.0))
            act.wait_ge(v_sum, 1)
            relu(0, 1024, 2)
            evacuate((KBT[:, 2:4, :], 0, 512, 1.0))
            evacuate((VBt[:, 0, :], 0, 512, 1.0))
            b_log(0)
            evacuate((VBt[:, 1, :], 0, 512, 1.0))
            b_exp(0)
            gate_half(6, 0)
            b_out(0)
            b_log(1)
            a_exp(SEQ, 1)
            gate_half(6, 1)
            b_exp(1)
            gate_half(7, 0)
            b_out(1)
            b_log(2)
            gate_half(7, 1)
            b_exp(2)
            gate_half(8, 0)
            b_out(2)
            b_log(3)
            a_exp(P, 2)
            gate_half(8, 1)
            b_exp(3)
            gate_half(9, 0)
            b_out(3)
            gate_half(9, 1)
            act.wait_ge(a_half, nh[0])
            for i in range(4):
                gi = G[:, 2 * i:2 * i + 2, :, :].rearrange("p c r t -> p (c r t)")
                A(gi, gi, ACT.Sigmoid).then_inc(a_sig, 1)
            for b in range(TB):
                act.wait_ge(m_xt, 4 + 2 * b)
                for k in range(4, KC):
                    A(XT[:, k, b * P:(b + 1) * P], Ap[:, 2 * b + 1, (k % 4) * P:(k % 4 + 1) * P], ACT.Copy,
                      scale=g_ffn[:, k:k + 1]).then_inc(a_xt, 1)
            for b in range(TB):
                act.wait_ge(v_tk, b + 1)
                A(G4[:, b, :], G4[:, b, :], ACT.Exp).then_inc(a_ge, 1)
            act.wait_ge(m_g, 1)
            A(GT, Bp[:, 0, 0:SEQ], ACT.Copy).then_inc(a_g, 1)

            def expert_block(n):
                act.wait_ge(d_gm, n)
                A(sg, gm, ACT.Sigmoid, scale=ALPHA).then_inc(a_sg, 1)
                act.wait_ge(m_y, n)
                A(ysb, Yps, ACT.Copy).then_inc(a_y, 1)
                act.wait_ge(m_gt, n + 1)
                A(GT, Gps[:, 0:SEQ], ACT.Copy).then_inc(a_gt, 1)

            act.wait_ge(v_rk, 1)
            act.sem_inc(a_gt, 1)
            act.sem_inc(a_y, 1)
            extra = act.alloc_register("act_extra")
            act.reg_mov(extra, 1)
            with act.Fori(0, NE) as e:
                count = act.value_load(CNT[0:1, bass.ds(e, 1)], min_val=0, max_val=SEQ)
                with act.If(count > SLOTS):
                    with act.Fori(1, SEQ // SLOTS) as j:
                        expert_block(act.snap(extra) + e + (j - 1))
                    act.reg_add(extra, extra, SEQ // SLOTS - 1)
                expert_block(act.snap(extra) + e)


_INS = ["x", "norm_mix_g", "w_in", "q_norm_g", "k_norm_g", "w_proj_a", "w_proj_b", "w_out", "norm_ffn_g",
        "w_router", "b_router", "w_gate_up", "b_gate_up", "w_down", "b_down"]


def kernel(**inputs):
    import concourse.bacc as bacc
    from concourse.bass_utils import run_bass_kernel_spmd

    nc = bacc.Bacc("TRN2", target_bir_lowering=False, num_devices=1)
    arrays, args = {}, []
    for name in _INS + ["consts"]:
        a = np.ascontiguousarray(inputs[name]) if name in inputs else shape_constants()
        arrays[f"in_{name}"] = a
        args.append(nc.dram_tensor(f"in_{name}", a.shape, mybir.dt.from_np(a.dtype), kind="ExternalInput").ap())
    args.append(nc.dram_tensor("out_h", (1, SEQ, D), F32, kind="ExternalOutput").ap())
    hybrid_block(nc, *args)
    r = run_bass_kernel_spmd(nc, [arrays], core_ids=[0])
    return r.results[0]["out_h"]
```
